# Optimizing a Trainium2 kernel written in Bass

```python
import jax, jax.numpy as jnp
from jax import lax
import numpy as np

D_MODEL = 1024
BATCH = 1
SEQ = 1024
DEPTH = 1

CHUNK = 64
EPS = 1e-6
D_MIX = D_MODEL
SB_HEADS = 8
SB_HEAD_DIM = 64
SB_WIDTH = SB_HEADS * SB_HEAD_DIM
SB_QBLOCK = 128
GDN_HEADS = 4
GDN_HEAD_DIM = 128
GDN_WIDTH = GDN_HEADS * GDN_HEAD_DIM
CONV_WIDTH = 4
SB_QKV_COLS = 3 * SB_WIDTH
GDN_QKV_COLS = 3 * GDN_WIDTH
GDN_GATE_COLS = GDN_WIDTH
IN_COLS = SB_QKV_COLS + GDN_QKV_COLS + GDN_GATE_COLS + 2 * GDN_HEADS
PEER_HEADS = 8
N_KEYS = 128
N_EXPERTS = N_KEYS * N_KEYS
PEER_TOPK = 16
PEER_QDIM = 256
PEER_HALF = PEER_QDIM // 2
PEER_TOKEN_BLOCK = 128

kernel_name = "hybrid_sbattn_gdn_peer_layer"

def rms_norm(x, w):
    xf = x.astype(jnp.float32)
    y = xf * lax.rsqrt(jnp.mean(xf * xf, axis=-1, keepdims=True) + EPS) * w.astype(jnp.float32)
    return y.astype(x.dtype)

def l2_normalize(x):
    return x * lax.rsqrt(jnp.sum(x * x, axis=-1, keepdims=True) + EPS)

def causal_depthwise_conv(x, w):
    c = x.shape[-1]
    return lax.conv_general_dilated(x, w[:, None, :], window_strides=(1,), padding=[(CONV_WIDTH - 1, 0)],
                                    dimension_numbers=('NWC', 'WIO', 'NWC'), feature_group_count=c)

def stick_breaking_attention(q, k, v):
    b, s, h, d = q.shape
    scale = d ** -0.5
    qh = jnp.transpose(q, (0, 2, 1, 3)).astype(jnp.float32)
    kh = jnp.transpose(k, (0, 2, 1, 3)).astype(jnp.float32)
    vh = jnp.transpose(v, (0, 2, 1, 3)).astype(jnp.float32)
    nb = s // SB_QBLOCK
    q_blocks = qh.reshape(b, h, nb, SB_QBLOCK, d).transpose(2, 0, 1, 3, 4)
    starts = jnp.arange(nb, dtype=jnp.int32) * SB_QBLOCK
    key_pos = jnp.arange(s, dtype=jnp.int32)

    def block(args):
        qb, start = args
        z = jnp.einsum('bhqd,bhkd->bhqk', qb, kh) * scale
        qpos = start + jnp.arange(SB_QBLOCK, dtype=jnp.int32)
        mask = key_pos[None, :] < qpos[:, None]
        log_keep = jnp.where(mask, jax.nn.log_sigmoid(-z), 0.0)
        log_after = lax.cumsum(log_keep, axis=3, reverse=True) - log_keep
        weights = jnp.where(mask, jnp.exp(jax.nn.log_sigmoid(z) + log_after), 0.0)
        return jnp.einsum('bhqk,bhkd->bhqd', weights, vh)

    out = lax.map(block, (q_blocks, starts))
    return out.transpose(1, 0, 3, 2, 4).reshape(b, s, h, d)

def gated_delta_net(q, k, v, g, beta):
    b, s, h, dk = q.shape
    dv = v.shape[-1]
    n = s // CHUNK

    def chunks(t):
        return t.reshape(b, n, CHUNK, h, t.shape[-1]).transpose(0, 3, 1, 2, 4)

    q, k, v = chunks(q), chunks(k), chunks(v)
    g = g.reshape(b, n, CHUNK, h).transpose(0, 3, 1, 2)
    beta = beta.reshape(b, n, CHUNK, h).transpose(0, 3, 1, 2)
    G = lax.cumsum(g, axis=3)
    idx = jnp.arange(CHUNK)
    causal = idx[:, None] >= idx[None, :]
    strict = idx[:, None] > idx[None, :]
    decay = jnp.exp(jnp.where(causal, G[..., :, None] - G[..., None, :], -jnp.inf))
    k_beta = k * beta[..., None]
    a_strict = jnp.where(strict, jnp.einsum('bhnid,bhnjd->bhnij', k_beta, k) * decay, 0.0)
    eye = jnp.eye(CHUNK, dtype=q.dtype)
    rhs = jnp.concatenate([v * beta[..., None], k_beta * jnp.exp(G)[..., None]], axis=-1)
    sol = lax.linalg.triangular_solve(a_strict + eye, rhs, left_side=True, lower=True, unit_diagonal=True)
    u, w = sol[..., :dv], sol[..., dv:]
    intra = jnp.einsum('bhnid,bhnjd->bhnij', q, k) * decay
    q_dec = q * jnp.exp(G)[..., None]
    g_last = G[..., -1]
    k_dec = k * jnp.exp(g_last[..., None] - G)[..., None]

    def step(state, xs):
        u_c, w_c, intra_c, q_c, k_c, gl = xs
        v_new = u_c - jnp.einsum('bhik,bhkv->bhiv', w_c, state)
        o = jnp.einsum('bhik,bhkv->bhiv', q_c, state) + jnp.einsum('bhij,bhjv->bhiv', intra_c, v_new)
        state = state * jnp.exp(gl)[..., None, None] + jnp.einsum('bhik,bhiv->bhkv', k_c, v_new)
        return state, o

    xs = tuple(jnp.moveaxis(t, 2, 0) for t in (u, w, intra, q_dec, k_dec, g_last))
    state0 = jnp.zeros((b, h, dk, dv), jnp.float32)
    _, o = lax.scan(step, state0, xs)
    return o.transpose(1, 0, 3, 2, 4).reshape(b, s, h, dv)

def peer_ffn(hn, w_q, sub_keys_1, sub_keys_2, u_table, v_table):
    b, s, d = hn.shape
    t = b * s
    ht = hn.reshape(t, d)
    q = (ht @ w_q).reshape(t, PEER_HEADS, PEER_QDIM).astype(jnp.float32)
    s1 = jnp.einsum('thd,hkd->thk', q[..., :PEER_HALF], sub_keys_1.astype(jnp.float32))
    s2 = jnp.einsum('thd,hkd->thk', q[..., PEER_HALF:], sub_keys_2.astype(jnp.float32))
    v1, i1 = lax.top_k(s1, PEER_TOPK)
    v2, i2 = lax.top_k(s2, PEER_TOPK)
    cand = (v1[..., :, None] + v2[..., None, :]).reshape(t, PEER_HEADS, PEER_TOPK * PEER_TOPK)
    best, ci = lax.top_k(cand, PEER_TOPK)
    e1 = jnp.take_along_axis(i1, ci // PEER_TOPK, axis=-1)
    e2 = jnp.take_along_axis(i2, ci % PEER_TOPK, axis=-1)
    experts = e1 * N_KEYS + e2
    gates = jax.nn.softmax(best, axis=-1)
    nb = t // PEER_TOKEN_BLOCK

    def block(args):
        xb, eb, gb = args
        u = u_table[eb]
        act = jax.nn.gelu(jnp.einsum('thkd,td->thk', u, xb).astype(jnp.float32)) * gb
        vv = v_table[eb]
        return jnp.einsum('thk,thkd->td', act.astype(vv.dtype), vv)

    out = lax.map(block, (ht.reshape(nb, PEER_TOKEN_BLOCK, d),
                          experts.reshape(nb, PEER_TOKEN_BLOCK, PEER_HEADS, PEER_TOPK),
                          gates.reshape(nb, PEER_TOKEN_BLOCK, PEER_HEADS, PEER_TOPK)))
    return out.reshape(b, s, d).astype(hn.dtype)

def hybrid_layer(x, norm1_w, w_in, sb_q_norm_w, sb_k_norm_w, sb_out_norm_w, gdn_conv_w, gdn_a_log,
                 gdn_dt_bias, gdn_out_norm_w, w_out, norm2_w, peer_w_q, peer_sub_keys_1, peer_sub_keys_2,
                 peer_u, peer_v):
    b, s, _ = x.shape
    h = rms_norm(x, norm1_w)
    proj = jnp.einsum('bsd,dc->bsc', h, w_in)
    sb_qkv, gdn_qkv, gdn_gate, gdn_a, gdn_b = jnp.split(
        proj, [SB_QKV_COLS, SB_QKV_COLS + GDN_QKV_COLS, SB_QKV_COLS + GDN_QKV_COLS + GDN_GATE_COLS,
               SB_QKV_COLS + GDN_QKV_COLS + GDN_GATE_COLS + GDN_HEADS], axis=-1)

    sq, sk, sv = [t.reshape(b, s, SB_HEADS, SB_HEAD_DIM) for t in jnp.split(sb_qkv, 3, axis=-1)]
    sq = rms_norm(sq, sb_q_norm_w)
    sk = rms_norm(sk, sb_k_norm_w)
    o_sb = stick_breaking_attention(sq, sk, sv)
    o_sb = rms_norm(o_sb, sb_out_norm_w.reshape(SB_HEADS, SB_HEAD_DIM)).reshape(b, s, SB_WIDTH)

    qkv = jax.nn.silu(causal_depthwise_conv(gdn_qkv.astype(jnp.float32), gdn_conv_w.astype(jnp.float32)))
    gq, gk, gv = [t.reshape(b, s, GDN_HEADS, GDN_HEAD_DIM) for t in jnp.split(qkv, 3, axis=-1)]
    gq = l2_normalize(gq) * (GDN_HEAD_DIM ** -0.5)
    gk = l2_normalize(gk)
    log_decay = -jnp.exp(gdn_a_log.astype(jnp.float32)) * jax.nn.softplus(
        gdn_a.astype(jnp.float32) + gdn_dt_bias.astype(jnp.float32))
    write = jax.nn.sigmoid(gdn_b.astype(jnp.float32))
    o_gdn = gated_delta_net(gq, gk, gv, log_decay, write)
    gate = jax.nn.silu(gdn_gate.astype(jnp.float32)).reshape(b, s, GDN_HEADS, GDN_HEAD_DIM)
    o_gdn = (rms_norm(o_gdn, gdn_out_norm_w) * gate).reshape(b, s, GDN_WIDTH)

    mix = jnp.concatenate([o_sb.astype(x.dtype), o_gdn.astype(x.dtype)], axis=-1)
    x = x + jnp.einsum('bsc,cd->bsd', mix, w_out)

    x = x + peer_ffn(rms_norm(x, norm2_w), peer_w_q, peer_sub_keys_1, peer_sub_keys_2, peer_u, peer_v)
    return x

def setup_inputs(seed: int = 0) -> dict:
    key = jax.random.key(seed)
    ks = jax.random.split(key, 18)
    f32 = jnp.float32
    nrm = lambda k, shape, sc: jax.random.normal(k, shape, f32) * sc
    dt = jnp.exp(jax.random.uniform(ks[8], (DEPTH, GDN_HEADS), f32, np.log(1e-3), np.log(1e-1)))
    return {
        "x": jax.random.normal(ks[0], (BATCH, SEQ, D_MODEL), f32),
        "norm1_w": 1.0 + nrm(ks[1], (DEPTH, D_MODEL), 0.02),
        "w_in": nrm(ks[2], (DEPTH, D_MODEL, IN_COLS), D_MODEL ** -0.5),
        "sb_q_norm_w": 1.0 + nrm(ks[3], (DEPTH, SB_HEAD_DIM), 0.02),
        "sb_k_norm_w": 1.0 + nrm(ks[4], (DEPTH, SB_HEAD_DIM), 0.02),
        "sb_out_norm_w": 1.0 + nrm(ks[5], (DEPTH, SB_WIDTH), 0.02),
        "gdn_conv_w": nrm(ks[6], (DEPTH, CONV_WIDTH, GDN_QKV_COLS), CONV_WIDTH ** -0.5),
        "gdn_a_log": jnp.log(jax.random.uniform(ks[7], (DEPTH, GDN_HEADS), f32, 1.0, 16.0)),
        "gdn_dt_bias": dt + jnp.log(-jnp.expm1(-dt)),
        "gdn_out_norm_w": 1.0 + nrm(ks[9], (DEPTH, GDN_HEAD_DIM), 0.02),
        "w_out": nrm(ks[10], (DEPTH, D_MIX, D_MODEL), D_MIX ** -0.5),
        "norm2_w": 1.0 + nrm(ks[11], (DEPTH, D_MODEL), 0.02),
        "peer_w_q": nrm(ks[12], (DEPTH, D_MODEL, PEER_HEADS * PEER_QDIM), D_MODEL ** -0.5),
        "peer_sub_keys_1": nrm(ks[13], (DEPTH, PEER_HEADS, N_KEYS, PEER_HALF), PEER_HALF ** -0.5),
        "peer_sub_keys_2": nrm(ks[14], (DEPTH, PEER_HEADS, N_KEYS, PEER_HALF), PEER_HALF ** -0.5),
        "peer_u": nrm(ks[15], (DEPTH, N_EXPERTS, D_MODEL), D_MODEL ** -0.5),
        "peer_v": nrm(ks[16], (DEPTH, N_EXPERTS, D_MODEL), PEER_TOPK ** -0.5),
    }

def reference(x, norm1_w, w_in, sb_q_norm_w, sb_k_norm_w, sb_out_norm_w, gdn_conv_w, gdn_a_log, gdn_dt_bias,
              gdn_out_norm_w, w_out, norm2_w, peer_w_q, peer_sub_keys_1, peer_sub_keys_2, peer_u, peer_v):
    for layer in range(DEPTH):
        x = hybrid_layer(x, norm1_w[layer], w_in[layer], sb_q_norm_w[layer], sb_k_norm_w[layer],
                         sb_out_norm_w[layer], gdn_conv_w[layer], gdn_a_log[layer], gdn_dt_bias[layer],
                         gdn_out_norm_w[layer], w_out[layer], norm2_w[layer], peer_w_q[layer],
                         peer_sub_keys_1[layer], peer_sub_keys_2[layer], peer_u[layer], peer_v[layer])
    return x


_drawn_inputs = setup_inputs


def setup_inputs(seed=0):
    import zlib

    import numpy as np

    out = dict(_drawn_inputs(seed))
    spreads = {}
    factors = {'sb_q_norm_w': 5.4,
     'sb_k_norm_w': 6.286,
     'sb_out_norm_w': 10.346,
     'gdn_out_norm_w': 15.937,
     'norm2_w': 13.164}
    for name, (base, spread) in spreads.items():
        noise = np.random.default_rng([zlib.crc32(name.encode()), seed]).standard_normal(out[name].shape)
        drawn = base * np.exp(spread * noise) if base else spread * noise
        out[name] = __import__('jax').numpy.asarray(drawn.astype(out[name].dtype))
    for name, factor in factors.items():
        out[name] = (out[name] * factor).astype(out[name].dtype)
    return out
```

```python
import math
from contextlib import ExitStack

import concourse.bass as bass
from concourse import mybir

F32 = mybir.dt.float32
BF16 = mybir.dt.bfloat16
U32 = mybir.dt.uint32
ALU = mybir.AluOpType
ACT = mybir.ActivationFunctionType
AX = mybir.AxisListType

P = 128
S, D = 1024, 1024
NB = S // P
KC = D // P
SBH, SBD = 8, 64
GH, GD = 4, 128
CHUNK = 64
TAPS = 4
SBW, GW = SBH * SBD, GH * GD
COL_SV = 2 * SBW
COL_G = 3 * SBW
COL_GATE = COL_G + 3 * GW
COL_AB = COL_GATE + GW
INC = COL_AB + 2 * GH
PH, NK, TOPK = 8, 128, 16
SLOTS = PH * TOPK
GS = 4
NG = SLOTS // GS
EPS = 1e-6
HALF = 512
NEG = -1e30
BIG = 3e38
GELU_C = 0.044715
GELU_S = math.sqrt(2.0 / math.pi)

CH = []
for _c in range(8):
    CH.append(("g", _c, COL_G + _c * P))
    CH.append(("s", _c, _c * P))
for _c in range(4):
    CH.append(("v", _c, COL_G + (8 + _c) * P))
NCH = len(CH)


def conv_count(n):
    return sum(k in "gv" for k, _, _ in CH[:n + 1])


def norm_count(n):
    return sum(k in "gs" for k, _, _ in CH[:n + 1])


def needs_tokens(n):
    return CH[n][0] == "v" or (CH[n][0] == "g" and CH[n][1] >= GH)


def token_count(n):
    return sum(needs_tokens(m) for m in range(n + 1))


def hybrid_layer_kernel(nc, x, norm1_w, w_in, sb_q_norm_w, sb_k_norm_w, sb_out_norm_w, gdn_conv_w,
                        gdn_a_log, gdn_dt_bias, gdn_out_norm_w, w_out, norm2_w, peer_w_q,
                        peer_sub_keys_1, peer_sub_keys_2, peer_u, peer_v, out):
    x_blk = x[0].rearrange("(n p) d -> n p d", p=P)
    out_blk = out[0].rearrange("(n p) d -> n p d", p=P)
    u_rows, v_rows = peer_u[0], peer_v[0]

    def scratch(name, shape):
        return nc.dram_tensor(name, shape, F32, kind="Internal").ap()

    d_qT = scratch("d_qT", (NB, P, 4, P))
    d_kT = scratch("d_kT", (NB, P, 4, P))
    d_v = scratch("d_v", (NB, P, SBW))
    d_gqT = scratch("d_gqT", (NB, P, GH, P))
    d_gkT = scratch("d_gkT", (NB, P, GH, P))
    d_gk = scratch("d_gk", (NB, P, GH, P))
    d_gv = scratch("d_gv", (NB, P, GH, P))
    d_gate = scratch("d_gate", (NB, P, GW))
    d_ab = scratch("d_ab", (NB, P, 2 * GH))
    d_subT = scratch("d_subT", (P, 2 * PH, NK))
    d_h = scratch("d_h", (NB, P, D))

    ctx = ExitStack()
    with ctx:
        def sb(name, shape, dt=F32):
            return ctx.enter_context(nc.sbuf_tensor(name, shape, dt))

        def sem(name):
            return ctx.enter_context(nc.semaphore(name))

        ident = sb("ident", [P, P])
        ones = sb("ones", [P, P])
        later = sb("later", [P, P])
        rest = sb("rest", [P, P])
        visible = sb("visible", [P, P], BF16)
        hidden = sb("hidden", [P, P], BF16)
        mean64 = sb("mean64", [P, P])
        upto = sb("upto", [P, P])
        levels = sb("levels", [P, 6, P], BF16)
        iota16 = sb("iota16", [P, TOPK])
        vecs = sb("vecs", [P, P])
        norm2b = sb("norm2b", [P, D])
        a_neg = sb("a_neg", [P, GH])
        dt_b = sb("dt_b", [P, GH])
        weights = sb("weights", [P, KC * INC])
        work = sb("work", [P, 20160])

        dots = sb("dots", [P, SLOTS])
        act_w = sb("act_w", [P, SLOTS])
        gate_cur = sb("gate_cur", [P, SLOTS])
        gate_new = sb("gate_new", [P, SLOTS])
        idx_new = sb("idx_new", [P, SLOTS], U32)
        idx_u = sb("idx_u", [P, SLOTS], U32)
        idx_v = sb("idx_v", [P, SLOTS], U32)
        stage_u = [sb(f"stage_u{p}", [P, GS], U32) for p in range(2)]
        stage_v = [sb(f"stage_v{p}", [P, GS], U32) for p in range(2)]
        gelu_t = sb("gelu_t", [P, SLOTS])
        diag = sb("diag", [P, GS, P])
        ab_in = sb("ab_in", [P, 2 * GH])
        sm = sb("sm", [P, 192])

        zz = ctx.enter_context(nc.psum_tensor("zz", [P, 2 * HALF], F32))
        rr = ctx.enter_context(nc.psum_tensor("rr", [P, 2 * HALF], F32))
        ox = ctx.enter_context(nc.psum_tensor("ox", [P, 2 * HALF], F32))
        va = ctx.enter_context(nc.psum_tensor("va", [P, 2 * HALF], F32))

        def bank(t, n):
            return t[:, n * HALF:(n + 1) * HALF]

        w_in_sb = weights[:, :].rearrange("p (k n) -> p k n", k=KC)
        xT = work[:, 0:KC * S].rearrange("p (k t) -> p k t", k=KC)
        x_all = work[:, 8192:8192 + NB * D].rearrange("p (n d) -> p n d", n=NB)
        sub_in = work[:, 16384:16384 + PH * NK].rearrange("p (h k) -> p h k", h=PH)
        sub_out = work[:, 17408:17408 + PH * NK].rearrange("p (h k) -> p h k", h=PH)
        vec_rows = work[:, 18432:18560]
        A0 = 8192

        def tile_a(n):
            return work[:, A0 + n * 512:A0 + (n + 1) * 512]

        s_ring = [tile_a(n) for n in range(6)]
        e_ring = [tile_a(6 + n) for n in range(2)]
        sq_ring = [tile_a(8 + n) for n in range(2)]
        y_ring = [tile_a(10 + n) for n in range(2)]
        o_ring = [tile_a(12 + n) for n in range(4)]
        tok_ring = [tile_a(16 + n) for n in range(2)]
        tmp_a = [tile_a(18), tile_a(19)]
        cb = [work[:, A0 + 10240 + n * 516:A0 + 10240 + n * 516 + 515] for n in range(2)]
        hist = work[:, A0 + 11280:A0 + 11280 + 36].rearrange("p (c k) -> p c k", c=12)
        mm_bank = [bank(zz, 0), bank(zz, 1)]
        ss_bank = [bank(rr, 0), bank(rr, 1), bank(ox, 0)]
        tr_bank = [bank(ox, 1), bank(va, 0)]
        stage_x = [work[:, A0 + n * 1024:A0 + (n + 1) * 1024].rearrange("p (k t) -> p k t", k=KC) for n in range(2)]
        v_out = [tile_a(4 + n) for n in range(2)]
        g_out = [tile_a(6 + n) for n in range(2)]
        g_exp = [tile_a(8 + n) for n in range(2)]
        ab_out = [work[:, A0 + 5120 + 16 * n:A0 + 5120 + 16 * n + 8] for n in range(2)]
        ab_y = [work[:, A0 + 5160 + 16 * n:A0 + 5160 + 16 * n + 4] for n in range(2)]
        ab_e = [work[:, A0 + 5200 + 16 * n:A0 + 5200 + 16 * n + 8] for n in range(2)]
        av_bank = [bank(zz, 0), bank(zz, 1)]
        ag_bank = [bank(rr, 0), bank(rr, 1)]
        ab_bank = [bank(ox, 0)[:, 0:8], bank(ox, 1)[:, 0:8]]

        w_q_sb = weights[:, 0:KC * 2048].rearrange("p (k n) -> p k n", k=KC)
        w_out_sb = weights[:, 16384:16384 + KC * D].rearrange("p (k n) -> p k n", k=KC)
        u_ring = weights[:, 24576:24576 + GS * D].rearrange("p (s d) -> p s d", s=GS)
        v_ring = work[:, 13824:13824 + GS * D].rearrange("p (s d) -> p s d", s=GS)
        hn_cur = work[:, 17920:17920 + D]
        y_buf = work[:, 18944:18944 + D]

        def T(n, m=1):
            return work[:, n * 512:(n + m) * 512]

        def heads(ap, h):
            return ap.rearrange("p (h c) -> p h c", h=h)

        gqT, gkT, gk, gv, gate = (T(n) for n in range(5))
        subT = heads(T(0, 4), 2 * PH)
        qT, kTj, vj = T(5), T(6), T(7)
        x_in = T(5, 2)
        W = 8
        t_xt, t_p = T(W), T(W + 1)
        t_dt, t_at, t_qd, t_vb, t_kbg, t_kd = (T(W + n) for n in range(2, 8))
        t_T, t_TT, t_u, t_wT, t_vn = (T(W + n) for n in range(8, 13))
        att_l, att_sp, att_u = [T(W), T(W + 3)], [T(W + 1), T(W + 4)], [T(W + 2), T(W + 5)]
        sq_att, sq_gdn = T(W + 6), T(W + 7)
        mixT = T(W, 2)
        h_sb = T(W + 2, 2)
        sq_h = T(W + 4, 2)
        hnT = T(W + 6, 2)
        pqT = heads(T(W + 8, 4), 2 * PH)
        sc = T(W, 4).rearrange("p (h c k) -> p h c k", h=PH, c=2)
        cand = T(W + 4, 4).rearrange("p (h i j) -> p h i j", h=PH, i=TOPK)
        hot = T(W + 8, 4).rearrange("p (h k j) -> p h k j", h=PH, k=TOPK)
        state = T(21)
        mix = T(22, 2)
        hn_new = mix
        small = work[:, 24 * 512:27 * 512]
        top_v = small[:, 0:256].rearrange("p (h c k) -> p h c k", h=PH, c=2)
        top_i = small[:, 256:512].bitcast(U32).rearrange("p (h c k) -> p h c k", h=PH, c=2)
        top_f = small[:, 512:768].rearrange("p (h c k) -> p h c k", h=PH, c=2)
        best = small[:, 768:896].rearrange("p (h k) -> p h k", h=PH)
        ci = small[:, 896:1024].bitcast(U32).rearrange("p (h k) -> p h k", h=PH)
        ci_hi = small[:, 1024:1152].bitcast(U32)
        ci_f = small[:, 1152:1280].rearrange("p (h k) -> p h k", h=PH)
        e1 = small[:, 1280:1408].rearrange("p (h k) -> p h k", h=PH)
        e2 = small[:, 1408:1536].rearrange("p (h k) -> p h k", h=PH)

        g_sel = sm[:, 0:8]
        ex_in = sm[:, 8:24]
        ex = sm[:, 24:40]
        kbg_w = sm[:, 40:44]
        ss12, ms12, y12, a12, r12 = (sm[:, 48 + 12 * n:60 + 12 * n] for n in range(5))
        ssh, msh, yh, ah, rh = (sm[:, 112 + n:113 + n] for n in range(5))
        ss8, ms8, y8, a8, r8 = (sm[:, 120 + 8 * n:128 + 8 * n] for n in range(5))
        gsum = sm[:, 160:168]

        consts = sem("consts")
        mask_step = sem("mask_step")
        consts_loaded = sem("consts_loaded")
        vec_clear, vec_turned, vecs_ready = sem("vec_clear"), sem("vec_turned"), sem("vecs_ready")
        vec_consts = sem("vec_consts")
        w_in_landed = [sem(f"w_in_landed{k}") for k in range(KC)]
        w_in_scaled = sem("w_in_scaled")
        w_in_scaled_act = sem("w_in_scaled_act")
        x_landed = [sem(f"x_landed{n}") for n in range(2)]
        x_squared, x_meaned, x_seeded, x_scaled = sem("x_squared"), sem("x_meaned"), sem("x_seeded"), sem("x_scaled")
        x_turned, xT_act, xT_dve = sem("x_turned"), sem("xT_act"), sem("xT_dve")
        sub_landed, sub_turned, sub_copied, sub_stored = (sem("sub_landed"), sem("sub_turned"),
                                                          sem("sub_copied"), sem("sub_stored"))
        projected, evacuated, convolved, exp_done = sem("projected"), sem("evacuated"), sem("convolved"), sem("exp_done")
        silu_done, squared, summed, seeded, normed = (sem("silu_done"), sem("squared"), sem("summed"),
                                                      sem("seeded"), sem("normed"))
        turned, turned_copied = sem("turned"), sem("turned_copied")
        o_stored = [sem(f"o_stored{n}") for n in range(4)]
        tok_stored = [sem(f"tok_stored{n}") for n in range(2)]
        x_staged, tok_projected = sem("x_staged"), sem("tok_projected")
        v_copied, gate_exp, gate_done, ab_sum, ab_exp, ab_done = (sem("v_copied"), sem("gate_exp"), sem("gate_done"),
                                                                   sem("ab_sum"), sem("ab_exp"), sem("ab_done"))
        a2_stored = [sem(f"a2_stored{n}") for n in range(2)]
        wq_landed, wout_landed, wout_scaled = sem("wq_landed"), sem("wout_landed"), sem("wout_scaled")
        gdn_landed = sem("gdn_landed")
        g_split, g_summed, ex_ready, ex_done = sem("g_split"), sem("g_summed"), sem("ex_ready"), sem("ex_done")
        diags_ready, spread_done, decay_arg, decay_exp = (sem("diags_ready"), sem("spread_done"),
                                                          sem("decay_arg"), sem("decay_exp"))
        qd_exp = sem("qd_exp")
        pairs_done, tt_first = sem("pairs_done"), sem("tt_first")
        x_ready, p_done, p_copied, corr_done, t_ready = (sem("x_ready"), sem("p_done"), sem("p_copied"),
                                                         sem("corr_done"), sem("t_ready"))
        tt_turned, tt_copied = sem("tt_turned"), sem("tt_copied")
        uw_done, uw_copied = sem("uw_done"), sem("uw_copied")
        ws_done, vn_ready, kv_done, state_ready = sem("ws_done"), sem("vn_ready"), sem("kv_done"), sem("state_ready")
        og_done, og_copied = sem("og_done"), sem("og_copied")

        q_landed = sem("q_landed")
        k_landed, vj_landed = sem("k_landed"), sem("vj_landed")
        z_done = [sem("z_done0"), sem("z_done1")]
        l_done = [sem("l_done0"), sem("l_done1")]
        sp_done = [sem("sp_done0"), sem("sp_done1")]
        z_used = [sem("z_used0"), sem("z_used1")]
        later_done = [sem("later_done0"), sem("later_done1")]
        arg_done = [sem("arg_done0"), sem("arg_done1")]
        rest_done = [sem("rest_done0"), sem("rest_done1")]
        w_done = [sem("w_done0"), sem("w_done1")]
        pv_done = [sem("pv_done0"), sem("pv_done1")]

        o_squared, o_meaned, o_seeded, mix_done = sem("o_squared"), sem("o_meaned"), sem("o_seeded"), sem("mix_done")
        mix_turned, mixT_act, mixT_dve, out_done = sem("mix_turned"), sem("mixT_act"), sem("mixT_dve"), sem("out_done")
        xb_landed, h_done, h_stored, h_squared, h_meaned, h_seeded = (sem("xb_landed"), sem("h_done"), sem("h_stored"),
                                                                      sem("h_squared"), sem("h_meaned"), sem("h_seeded"))
        hn_done, hn_turned, hnT_act, hnT_dve = sem("hn_done"), sem("hn_turned"), sem("hnT_act"), sem("hnT_dve")
        pq_done, pq_copied, sub_in_b = sem("pq_done"), sem("pq_copied"), sem("sub_in_b")
        sc_done, sc_copied = sem("sc_done"), sem("sc_copied")
        best_shifted, best_exp, topk_done = sem("best_shifted"), sem("best_exp"), sem("topk_done")

        idx_moved, idx_staged, idx_step = sem("idx_moved"), sem("idx_staged"), sem("idx_step")
        u_landed = [sem(f"u_landed{k}") for k in range(GS)]
        v_landed = [sem(f"v_landed{k}") for k in range(GS)]
        dotted = sem("dotted")
        v_used = sem("v_used")
        diag_done = sem("diag_done")
        gelu_arg, gelu_exp, act_done = sem("gelu_arg"), sem("gelu_exp"), sem("act_done")
        h_back, y_done, y_stored = sem("h_back"), sem("y_done"), sem("y_stored")

        n1w = vecs[:, 0:8]
        R_OUT, R_CONV, R_GOUT, R_Q, R_K = 8, 12, 60, 61, 62
        vec_loads = [(vec_rows[0:8, :], norm1_w[0].rearrange("(k p) -> k p", p=P)),
                     (vec_rows[R_OUT:R_OUT + 4, :], sb_out_norm_w[0].rearrange("(k p) -> k p", p=P)),
                     (vec_rows[R_CONV:R_CONV + 48, :], gdn_conv_w[0].rearrange("k (c p) -> (k c) p", p=P)),
                     (vec_rows[R_GOUT:R_GOUT + 1, :], gdn_out_norm_w[0:1, :]),
                     (vec_rows[R_Q:R_Q + 1, 0:64], sb_q_norm_w[0:1, :]), (vec_rows[R_Q:R_Q + 1, 64:128], sb_q_norm_w[0:1, :]),
                     (vec_rows[R_K:R_K + 1, 0:64], sb_k_norm_w[0:1, :]), (vec_rows[R_K:R_K + 1, 64:128], sb_k_norm_w[0:1, :]),
                     (dt_b[:, :], gdn_dt_bias[0:1, :].to_broadcast([P, GH])),
                     (a_neg[:, :], gdn_a_log[0:1, :].to_broadcast([P, GH])),
                     (norm2b[:, :], norm2_w[0:1, :].to_broadcast([P, D]))]

        block = ctx.enter_context(nc.Block())

        def known(e):
            e.wait_ge(consts, 1)

        def settled(e, value):
            if not isinstance(value, int):
                value = e.snap(value)
                e.compute_val(value)
            return value

        def steps_before(b):
            return b * (b + 1) // 2

        @block.sync
        def _(sp):
            for n in range(2):
                sp.dma_start(x_all[:, 4 * n:4 * n + 4, :],
                             x_blk[4 * n:4 * n + 4].rearrange("n p d -> p n d")).then_inc(x_landed[n], 16)
            sp.wait_ge(vec_clear, 1)
            for dst, src in vec_loads:
                sp.dma_start(dst, src).then_inc(consts_loaded, 16)
            for n, keys in enumerate((peer_sub_keys_1, peer_sub_keys_2)):
                if n:
                    sp.wait_ge(sub_turned, 1)
                sp.dma_start(sub_in, keys[0].rearrange("h k d -> k h d")).then_inc(sub_landed, 16)
                sp.wait_ge(sub_copied, n + 1)
                sp.dma_start(d_subT.rearrange("p (h c) k -> p h c k", c=2)[:, :, n, :], sub_out).then_inc(sub_stored, 16)
                sp.wait_ge(sub_stored, 16 * (n + 1))
            with sp.Fori(0, 2) as half:
                for n in range(NCH + 2):
                    m = n - 2
                    if m >= 0 and needs_tokens(m):
                        t = token_count(m) - 1
                        dst = d_gv if CH[m][0] == "v" else d_gk
                        sp.wait_ge(turned_copied, 8 * half + t + 1)
                        sp.dma_start(dst[bass.ds(half * 4, 4), :, CH[m][1] % 4, :].rearrange("b t c -> t b c"),
                                     tok_ring[t % 2].rearrange("p (b c) -> p b c", b=4)).then_inc(tok_stored[t % 2], 16)
                    if n < NCH and CH[n][0] != "v":
                        kind, c, _ = CH[n]
                        dst = {("g", 0): d_gqT, ("g", 1): d_gkT, ("s", 0): d_qT, ("s", 1): d_kT}[kind, c // 4]
                        sp.wait_ge(normed, NCH * half + n + 1)
                        sp.dma_start(dst[bass.ds(half * 4, 4), :, c % 4, :].rearrange("b p t -> p b t"),
                                     o_ring[n % 4].rearrange("p (b t) -> p b t", b=4)).then_inc(o_stored[n % 4], 16)
            with sp.Fori(0, NB // 2) as pr:
                a0 = pr * 2
                for p in range(2):
                    sp.wait_ge(v_copied, a0 + p + 1)
                    sp.dma_start(d_v[a0 + p], v_out[p]).then_inc(a2_stored[p], 16)
                    sp.wait_ge(gate_done, a0 + p + 1)
                    sp.dma_start(d_gate[a0 + p], g_out[p]).then_inc(a2_stored[p], 16)
                    sp.wait_ge(ab_done, a0 + p + 1)
                    sp.dma_start(d_ab[a0 + p], ab_out[p]).then_inc(a2_stored[p], 16)
            sp.wait_ge(tok_projected, NB)
            sp.dma_start(w_q_sb, peer_w_q[0].rearrange("(k p) n -> p k n", p=P)).then_inc(wq_landed, 16)
            sp.dma_start(w_out_sb, w_out[0].rearrange("(k p) n -> p k n", p=P)).then_inc(wout_landed, 16)
            for n in range(4):
                sp.wait_ge(o_stored[n], 16 * 8)
            for n in range(2):
                sp.wait_ge(tok_stored[n], 16 * 8)
                sp.wait_ge(a2_stored[n], 16 * 12)

            def mix_loads(b):
                t0 = steps_before(b)
                known(sp)
                sp.wait_ge(mix_done, b)
                sp.wait_ge(sc_done, 4 * b)
                for dst, src in ((ab_in[:, :], d_ab), (gkT, d_gkT), (gqT, d_gqT), (gk, d_gk), (gv, d_gv)):
                    s2 = src[b] if len(src.shape) == 3 else src[b].rearrange("p h c -> p (h c)")
                    sp.dma_start(dst, s2).then_inc(gdn_landed, 16)
                sp.dma_start(gate, d_gate[b]).then_inc(gdn_landed, 16)
                sp.wait_ge(h_done, b)
                sp.dma_start(qT, d_qT[b].rearrange("p h c -> p (h c)")).then_inc(q_landed, 16)

                def key_block(t, j):
                    sp.wait_ge(z_done[0], t)
                    sp.wait_ge(z_done[1], t)
                    sp.dma_start(kTj, d_kT[j].rearrange("p h c -> p (h c)")).then_inc(k_landed, 16)
                    sp.wait_ge(pv_done[0], t)
                    sp.wait_ge(pv_done[1], t)
                    sp.dma_start(vj, d_v[j]).then_inc(vj_landed, 16)

                key_block(t0, b)
                return key_block, t0

            def mix_tail(b):
                t1 = steps_before(b + 1)
                sp.wait_ge(z_done[0], t1)
                sp.wait_ge(z_done[1], t1)
                sp.dma_start(x_in, x_blk[b]).then_inc(xb_landed, 16)
                sp.wait_ge(mix_done, b + 1)
                sp.dma_start(T(0, 4), d_subT.rearrange("p h k -> p (h k)")).then_inc(sub_in_b, 16)
                sp.wait_ge(h_done, b + 1)
                sp.dma_start(d_h[b], h_sb).then_inc(h_stored, 16)

            def h_reload(n):
                sp.dma_start(y_buf, d_h[n]).then_inc(h_back, 16)

            def y_store(n):
                sp.wait_ge(y_done, n + 1)
                sp.dma_start(out_blk[n], y_buf).then_inc(y_stored, 16)

            for i in range(2):
                key_block, t0 = mix_loads(i)
                for t in range(1, i + 1):
                    key_block(t0 + t, i - t)
                mix_tail(i)
            with sp.Fori(2, NB) as i:
                sp.wait_ge(h_stored, 16 * (i - 1))
                sp.wait_ge(y_stored, 16 * (i - 2))
                h_reload(i - 2)
                key_block, t0 = mix_loads(i)
                with sp.Fori(1, i + 1) as t:
                    key_block(t0 + t, nc.s_assert_within(
                        i - t, 0, NB - 1, skip_runtime_bounds_check_because="t runs from 1 to i"))
                mix_tail(i)
                y_store(i - 2)
            for i in range(NB, NB + 2):
                sp.wait_ge(h_stored, 16 * NB)
                sp.wait_ge(y_stored, 16 * (i - 2))
                h_reload(i - 2)
                y_store(i - 2)
            sp.wait_ge(y_stored, 16 * NB)

        @block.gpsimd
        def _(pool):
            g = nc.gpsimd
            g.memset(ident[:, :], 0.0)
            g.memset(ones[:, :], 1.0)
            g.memset(later[:, :], 1.0)
            g.memset(rest[:, :], 1.0)
            g.memset(visible[:, :], 1.0)
            g.memset(hidden[:, :], NEG)
            g.memset(upto[:, :], 1.0)
            g.memset(levels[:, :, :], 0.0)
            g.memset(mean64[:, :], 1.0 / SBD).then_inc(mask_step, 1)
            pool.wait_ge(mask_step, 1)
            for lv in range(6):
                s = 1 << lv
                g.memset(levels[:, lv, :].rearrange("p (a c) -> p a c", c=2 * s)[:, :, s:2 * s], 1.0)
            g.iota(iota16[:, :], [[1, TOPK]], base=0, channel_multiplier=0,
                   allow_small_or_imprecise_dtypes=True).then_inc(mask_step, 1)
            pool.wait_ge(mask_step, 2)

            def select(m, op, base, pattern, cm, fill=0.0):
                return g.affine_select(out=m, in_=m, compare_op=op, fill=fill, base=base, pattern=pattern,
                                       channel_multiplier=cm)

            select(ident[:, :], ALU.not_equal, 0, [[-1, P]], 1, 1.0)
            select(later[:, :], ALU.is_gt, 0, [[-1, P]], 1)
            select(rest[:, :], ALU.is_ge, 0, [[1, P]], -1)
            select(visible[:, :], ALU.is_gt, 0, [[1, P]], -1)
            select(hidden[:, :], ALU.is_ge, 0, [[-1, P]], 1)
            select(upto[:, :], ALU.is_ge, 0, [[1, P]], -1)
            select(mean64[:, 0:64], ALU.is_ge, 63, [[0, 64]], -1)
            select(mean64[:, 64:128], ALU.is_ge, -64, [[0, 64]], 1)
            for lv in range(6):
                s = 1 << lv
                m = levels[:, lv, :].rearrange("p (a c) -> p a c", c=2 * s)[:, :, s:2 * s]
                last = select(m, ALU.is_ge, 0, [[-2 * s, P // (2 * s)], [0, s]], 1)
            last.then_inc(mask_step, 1)
            pool.wait_ge(mask_step, 3)
            select(upto[:, 64:128], ALU.is_ge, -64, [[0, 64]], 1)
            for lv in range(6):
                s = 1 << lv
                m = levels[:, lv, :].rearrange("p (a c) -> p a c", c=2 * s)[:, :, s:2 * s]
                last = select(m, ALU.is_ge, s - 1, [[2 * s, P // (2 * s)], [0, s]], -1)
            last.then_inc(consts, 1)

            def gathers(i, do_u, do_v):
                if do_v:
                    count = settled(pool, i - 1)
                    known(pool)
                    pool.wait_ge(idx_moved, count)
                    mv = nc.gpsimd.tensor_copy(idx_v[:, :], idx_u[:, :])
                    if not do_u:
                        mv.then_inc(idx_moved, 1)
                if do_u:
                    if do_v:
                        mv.then_inc(idx_step, 1)
                        count = settled(pool, i - 1)
                        known(pool)
                        pool.wait_ge(idx_step, count)
                    else:
                        known(pool)
                    pool.wait_ge(topk_done, i)
                    nc.gpsimd.tensor_copy(idx_u[:, :], idx_new[:, :]).then_inc(idx_moved, 1)
                known(pool)
                pool.wait_ge(idx_moved, i)
                with pool.Fori(0, NG // 2) as pr:
                    g0 = pr * 2
                    for p in range(2):
                        gg = g0 + p
                        if do_u:
                            c = nc.gpsimd.tensor_copy(stage_u[p][:, :], idx_u[:, bass.ds(gg * GS, GS)])
                        if do_v:
                            c = nc.gpsimd.tensor_copy(stage_v[p][:, :], idx_v[:, bass.ds(gg * GS, GS)])
                        c.then_inc(idx_staged, 1)
                        pool.wait_ge(idx_staged, NG * (i - 1) + gg + 1)
                        for k in range(GS):
                            if do_u:
                                count = settled(pool, GS * (NG * (i - 1) + gg) + k + 1)
                                known(pool)
                                pool.wait_ge(dotted, count)
                                nc.gpsimd.indirect_dma_start(
                                    u_ring[:, k, :], None, u_rows,
                                    bass.IndirectOffsetOnAxis(stage_u[p][:, k:k + 1], 0)).then_inc(u_landed[k], 16)
                            if do_v:
                                count = settled(pool, GS * (NG * (i - 2) + gg) + k + 1)
                                known(pool)
                                pool.wait_ge(v_used, count)
                                nc.gpsimd.indirect_dma_start(
                                    v_ring[:, k, :], None, v_rows,
                                    bass.IndirectOffsetOnAxis(stage_v[p][:, k:k + 1], 0)).then_inc(v_landed[k], 16)

            gathers(1, True, False)
            with pool.Fori(2, NB) as i:
                gathers(i, True, True)
            gathers(NB, True, True)
            gathers(NB + 1, False, True)

        @block.scalar
        def _(act):
            a = nc.scalar
            for k in range(KC):
                act.dma_start(w_in_sb[:, k, :], w_in[0, k * P:(k + 1) * P, :]).then_inc(w_in_landed[k], 16)
            act.preload_act_table_set("natural_log_exp_and_others")
            for n in range(NB):
                if n % 4 == 0:
                    act.wait_ge(x_landed[n // 4], 16)
                if n:
                    act.drain()
                a.activation(y_buf, x_all[:, n, :], ACT.Square, accum_out=ss8[:, n:n + 1])
            act.drain()
            a.activation(y8[:, 0:1], ss8[:, 0:1], ACT.Copy).then_inc(x_squared, 1)
            act.wait_ge(x_meaned, 1)
            a.activation(y8, ms8, ACT.Ln)
            act.drain()
            a.activation(y8, y8, ACT.Exp, scale=-0.5).then_inc(x_seeded, 1)
            act.wait_ge(consts_loaded, 16 * len(vec_loads))
            a.activation(a_neg[:, :], a_neg[:, :], ACT.Exp).then_inc(vec_consts, 1)
            for n in range(NB):
                act.wait_ge(x_turned, n + 1)
                a.activation(xT[:, 0:4, n * P:(n + 1) * P], heads(bank(zz if n % 2 == 0 else rr, 0), 4),
                             ACT.Copy).then_inc(xT_act, 1)
            for n in range(2):
                act.wait_ge(sub_turned, n + 1)
                if n:
                    act.wait_ge(sub_stored, 16)
                a.activation(sub_out, heads(ox[:, :], PH), ACT.Copy).then_inc(sub_copied, 1)
            act.wait_ge(vecs_ready, 1)
            for k in range(1, KC, 2):
                act.wait_ge(w_in_landed[k], 16)
                a.activation(w_in_sb[:, k, :], w_in_sb[:, k, :], ACT.Copy, scale=n1w[:, k:k + 1]).then_inc(w_in_scaled_act, 1)
            with act.Fori(0, 2) as half:
                act.wait_ge(normed, NCH * half)
                for n in range(NCH + 8):
                    if n < NCH:
                        act.wait_ge(projected, NCH * half + n + 1)
                        if CH[n][0] == "s":
                            if n >= 6:
                                act.wait_ge(normed, NCH * half + n - 5)
                            a.activation(s_ring[n % 6], mm_bank[n % 2], ACT.Copy).then_inc(evacuated, 1)
                        else:
                            c = conv_count(n) - 1
                            if c >= 2:
                                act.wait_ge(convolved, 12 * half + c - 1)
                            a.activation(cb[c % 2][:, 3:515], mm_bank[n % 2], ACT.Copy).then_inc(evacuated, 1)
                    m = n - 1
                    if 0 <= m < NCH and CH[m][0] != "s":
                        c = conv_count(m) - 1
                        act.wait_ge(convolved, 12 * half + c + 1)
                        a.activation(e_ring[c % 2], s_ring[m % 6], ACT.Exp, scale=-1.0).then_inc(exp_done, 1)
                    m = n - 2
                    if 0 <= m < NCH and CH[m][0] != "v":
                        c = norm_count(m) - 1
                        if CH[m][0] == "g":
                            act.wait_ge(silu_done, 12 * half + conv_count(m))
                        else:
                            act.drain()
                        if c >= 2:
                            act.wait_ge(summed, 16 * half + c - 1)
                        a.activation(sq_ring[c % 2], s_ring[m % 6], ACT.Square).then_inc(squared, 1)
                    m = n - 4
                    if 0 <= m < NCH and CH[m][0] != "v":
                        c = norm_count(m) - 1
                        act.wait_ge(summed, 16 * half + c + 1)
                        if c >= 2:
                            act.wait_ge(normed, NCH * half + m - 1)
                        a.activation(y_ring[c % 2], ss_bank[c % 3], ACT.Ln, bias=EPS)
                        act.drain()
                        a.activation(y_ring[c % 2], y_ring[c % 2], ACT.Exp, scale=-0.5).then_inc(seeded, 1)
                    m = n - 7
                    if 0 <= m < NCH and needs_tokens(m):
                        t = token_count(m) - 1
                        act.wait_ge(turned, 8 * half + t + 1)
                        act.wait_ge(tok_stored[t % 2], 16 * (4 * half + t // 2))
                        a.activation(tok_ring[t % 2], tr_bank[t % 2], ACT.Copy).then_inc(turned_copied, 1)
            act.wait_ge(normed, 2 * NCH)
            for n in range(4):
                act.wait_ge(o_stored[n], 16 * 8)
            for n in range(2):
                act.wait_ge(tok_stored[n], 16 * 8)
            with act.Fori(0, NB // 2) as pr:
                a0 = pr * 2
                act.wait_ge(tok_projected, a0)
                known(act)
                for p in range(2):
                    a.activation(stage_x[p], xT[:, :, bass.ds((a0 + p) * P, P)], ACT.Copy).then_inc(x_staged, 1)
                for p in range(2):
                    act.wait_ge(a2_stored[p], 24 * a0)
                    act.wait_ge(tok_projected, a0 + p + 1)
                    a.activation(v_out[p], av_bank[p], ACT.Copy).then_inc(v_copied, 1)
                    a.activation(g_exp[p], ag_bank[p], ACT.Exp, scale=-1.0)
                    a.activation(ab_e[p][:, 4:8], ab_bank[p][:, 4:8], ACT.Exp, scale=-1.0).then_inc(gate_exp, 1)
                    act.wait_ge(ab_sum, a0 + p + 1)
                    a.activation(ab_e[p][:, 0:4], ab_e[p][:, 0:4], ACT.Exp)
                    act.drain()
                    a.activation(ab_e[p][:, 0:4], ab_e[p][:, 0:4], ACT.Ln, bias=1.0).then_inc(ab_exp, 1)

            def fill(i, g, v):
                if not v:
                    return
                for k in range(GS):
                    n = GS * (NG * (i - 2) + g) + k + 1
                    act.wait_ge(v_used, n)
                    known(act)
                    a.activation(diag[:, k, :], ident[:, :], ACT.Copy,
                                 scale=act_w[:, bass.ds(g * GS + k, 1)]).then_inc(diag_done, 1)

            def seed(y, ms, s):
                a.activation(y, ms, ACT.Ln)
                act.drain()
                a.activation(y, y, ACT.Exp, scale=-0.5).then_inc(s, 1)

            def mixing(b, i, v, loop):
                t0 = steps_before(b)
                act.wait_ge(ex_ready, b + 1)
                a.activation(ex, ex_in, ACT.Exp).then_inc(ex_done, 1)
                act.wait_ge(spread_done, b + 1)
                a.activation(t_qd, bank(zz, 0), ACT.Exp).then_inc(qd_exp, 1)
                act.wait_ge(decay_arg, b + 1)
                a.activation(t_dt, t_dt, ACT.Exp).then_inc(decay_exp, 1)
                act.wait_ge(tt_turned, b + 1)
                a.activation(t_T, bank(ox, 1), ACT.Copy).then_inc(tt_copied, 1)
                fill(i, 0, v)
                for lv in range(1, 6):
                    act.wait_ge(p_done, 5 * b + lv)
                    a.activation(t_p, bank(zz, 0), ACT.Copy).then_inc(p_copied, 1)
                    fill(i, lv, v)
                act.wait_ge(uw_done, b + 1)
                a.activation(t_u, bank(rr, 1), ACT.Copy)
                a.activation(t_wT, bank(ox, 1), ACT.Copy).then_inc(uw_copied, 1)
                fill(i, 6, v)
                fill(i, 7, v)
                act.wait_ge(og_done, b + 1)
                a.activation(mix[:, 512:1024], bank(ox, 0), ACT.Copy).then_inc(og_copied, 1)

                def key_step(t, g):
                    for hg in range(2):
                        act.wait_ge(z_done[hg], t + 1)
                        a.activation(att_l[hg], bank(zz, hg), ACT.Abs)
                        act.drain()
                        a.activation(att_l[hg], att_l[hg], ACT.Exp, scale=-1.0)
                        act.drain()
                        a.activation(att_l[hg], att_l[hg], ACT.Ln, bias=1.0).then_inc(l_done[hg], 1)
                    fill(i, g, v)
                    for hg in range(2):
                        act.wait_ge(arg_done[hg], t + 1)
                        a.activation(att_u[hg], att_u[hg], ACT.Exp).then_inc(w_done[hg], 1)

                key_step(t0, 8)
                loop(act, b, lambda t: key_step(t0 + t, 8 + t))
                for hg in range(2):
                    act.wait_ge(pv_done[hg], t0 + b + 1)
                a.activation(sq_att, bank(ox, 0), ACT.Square)
                a.activation(sq_gdn, mix[:, 512:1024], ACT.Square).then_inc(o_squared, 1)
                act.wait_ge(o_meaned, b + 1)
                seed(y12, ms12, o_seeded)
                g = 9 + b
                fill(i, g, v)
                act.wait_ge(mix_turned, b + 1)
                a.activation(mixT[:, 0:512], bank(rr, 0), ACT.Copy).then_inc(mixT_act, 1)
                fill(i, g + 1, v)
                act.wait_ge(h_done, b + 1)
                a.activation(sq_h, h_sb, ACT.Square, accum_out=ssh)
                act.drain()
                a.activation(yh, ssh, ACT.Copy).then_inc(h_squared, 1)
                act.wait_ge(h_meaned, b + 1)
                seed(yh, msh, h_seeded)
                fill(i, g + 2, v)
                act.wait_ge(hn_turned, b + 1)
                a.activation(hnT[:, 0:512], bank(rr, 0), ACT.Copy).then_inc(hnT_act, 1)
                for q in range(4):
                    act.wait_ge(pq_done, 4 * b + q + 1)
                    a.activation(pqT[:, 4 * q:4 * q + 4, :], heads(bank(zz if q < 2 else rr, q % 2), 4),
                                 ACT.Copy).then_inc(pq_copied, 1)
                    fill(i, g + 3 + q, v)
                act.wait_ge(h_stored, 16 * (b + 1))
                for q in range(4):
                    act.wait_ge(sc_done, 4 * b + q + 1)
                    a.activation(sc[:, 2 * q:2 * q + 2, :, :],
                                 bank(zz if q < 2 else rr, q % 2).rearrange("p (h c k) -> p h c k", h=2, c=2),
                                 ACT.Copy).then_inc(sc_copied, 1)
                for q in range(7):
                    fill(i, g + 7 + q, v)
                act.wait_ge(best_shifted, b + 1)
                a.activation(best, best, ACT.Exp).then_inc(best_exp, 1)
                return g + 14

            def ending(i, u):
                if u:
                    act.wait_ge(gelu_arg, i)
                    a.activation(gelu_t[:, :], gelu_t[:, :], ACT.Exp, scale=-2.0 * GELU_S).then_inc(gelu_exp, 1)

            def rest_groups(i, g, v):
                with act.Fori(g, NG) as gg:
                    fill(i, gg, v)

            def py_loop(e, b, body):
                for t in range(1, b + 1):
                    body(t)

            def fori_loop(e, b, body):
                with e.Fori(1, b + 1) as t:
                    body(t)

            mixing(0, 0, False, py_loop)
            mixing(1, 1, False, py_loop)
            ending(1, True)
            with act.Fori(2, NB) as i:
                act.wait_ge(act_done, i - 1)
                g = mixing(i, i, True, fori_loop)
                rest_groups(i, g, True)
                ending(i, True)
            act.wait_ge(act_done, NB - 1)
            rest_groups(NB, 0, True)
            ending(NB, True)
            act.wait_ge(act_done, NB)
            rest_groups(NB + 1, 0, True)

        @block.vector
        def _(dve):
            v = nc.vector

            def spread(ap, h, n):
                return ap.unsqueeze(2).to_broadcast([P, h, n])

            def every(ap, h):
                return ap.unsqueeze(1).to_broadcast([P, h, ap.shape[1]])

            def newton(r, y, ms, a):
                v.tensor_tensor(a, y, y, ALU.mult)
                dve.drain()
                v.tensor_tensor(a, a, ms, ALU.mult)
                dve.drain()
                v.scalar_tensor_tensor(r, a, -3.0, y, ALU.add, ALU.mult)
                dve.drain()

            def one_over_one_plus(e):
                v.tensor_scalar(e, e, 1.0, BIG, ALU.add, ALU.min)
                dve.drain()
                v.reciprocal(e, e)
                dve.drain()

            v.memset(vec_rows, 0.0).then_inc(vec_clear, 1)
            dve.wait_ge(x_squared, 1)
            v.memset(hist, 0.0).then_inc(dotted, GS)
            v.tensor_scalar(ms8, ss8, 1.0 / D, EPS, ALU.mult, ALU.add).then_inc(x_meaned, 1)
            dve.wait_ge(x_seeded, 1)
            newton(r8, y8, ms8, a8)
            for n in range(NB):
                v.tensor_scalar(x_all[:, n, :], x_all[:, n, :], r8[:, n:n + 1], -0.5, ALU.mult, ALU.mult).then_inc(x_scaled, 1)
            for n in range(NB):
                dve.wait_ge(x_turned, n + 1)
                v.tensor_copy(xT[:, 4:8, n * P:(n + 1) * P], heads(bank(zz if n % 2 == 0 else rr, 1), 4)).then_inc(xT_dve, 1)
            dve.wait_ge(vec_turned, 1)
            v.tensor_copy(vecs[:, :], bank(va, 1)[:, 0:P])
            dve.drain()
            v.tensor_scalar(vecs[:, R_Q:R_Q + 1], vecs[:, R_Q:R_Q + 1], -0.5 * SBD ** -0.5, None, ALU.mult)
            v.tensor_scalar(vecs[:, R_K:R_K + 1], vecs[:, R_K:R_K + 1], -0.5, None, ALU.mult).then_inc(vecs_ready, 1)
            for k in range(0, KC, 2):
                dve.wait_ge(w_in_landed[k], 16)
                v.tensor_scalar(w_in_sb[:, k, :], w_in_sb[:, k, :], n1w[:, k:k + 1], None, ALU.mult).then_inc(w_in_scaled, 1)
            dve.wait_ge(sub_stored, 32)
            with dve.Fori(0, 2) as half:
                for n in range(NCH + 8):
                    if n < NCH and CH[n][0] != "s":
                        c = conv_count(n) - 1
                        w = [R_CONV + 12 * k + CH[n][1] + (8 if CH[n][0] == "v" else 0) for k in range(TAPS)]
                        dve.wait_ge(evacuated, NCH * half + n + 1)
                        v.tensor_copy(cb[c % 2][:, 0:3], hist[:, c, :])
                        dve.drain()
                        v.tensor_copy(hist[:, c, :], cb[c % 2][:, 512:515])
                        v.tensor_scalar(s_ring[n % 6], cb[c % 2][:, 3:515], vecs[:, w[3]:w[3] + 1], None, ALU.mult)
                        for k in (2, 1, 0):
                            dve.drain()
                            last = v.scalar_tensor_tensor(s_ring[n % 6], cb[c % 2][:, k:k + 512], vecs[:, w[k]:w[k] + 1],
                                                          s_ring[n % 6], ALU.mult, ALU.add)
                        last.then_inc(convolved, 1)
                    m = n - 1
                    if 0 <= m < NCH and CH[m][0] != "s":
                        c = conv_count(m) - 1
                        dve.wait_ge(exp_done, 12 * half + c + 1)
                        one_over_one_plus(e_ring[c % 2])
                        v.tensor_tensor(s_ring[m % 6], s_ring[m % 6], e_ring[c % 2], ALU.mult).then_inc(silu_done, 1)
                    m = n - 5
                    if 0 <= m < NCH:
                        kind, ck, _ = CH[m]
                        if kind != "v":
                            c = norm_count(m) - 1
                            y, t0, t1 = y_ring[c % 2], tmp_a[0], tmp_a[1]
                            dve.drain()
                            dve.wait_ge(seeded, 16 * half + c + 1)
                            v.tensor_tensor(t0, y, y, ALU.mult)
                            dve.drain()
                            v.scalar_tensor_tensor(t1, ss_bank[c % 3], EPS, t0, ALU.add, ALU.mult)
                            dve.drain()
                            v.scalar_tensor_tensor(t0, t1, -3.0, y, ALU.add, ALU.mult)
                            scale = (vecs[:, R_Q + ck // 4:R_Q + ck // 4 + 1] if kind == "s"
                                     else -0.5 * (GD ** -0.5 if ck < GH else 1.0))
                        dve.drain()
                        dve.wait_ge(o_stored[m % 4], 16 * (4 * half + m // 4))
                        if m < 4:
                            dve.wait_ge(turned, 8 * half)
                        elif needs_tokens(m - 4):
                            dve.wait_ge(turned, 8 * half + token_count(m - 4))
                        if kind != "v":
                            v.scalar_tensor_tensor(o_ring[m % 4], s_ring[m % 6], scale, t0, ALU.mult, ALU.mult).then_inc(normed, 1)
                        else:
                            v.tensor_copy(o_ring[m % 4], s_ring[m % 6]).then_inc(normed, 1)
            dve.wait_ge(vec_consts, 1)
            dve.wait_ge(turned_copied, 16)
            with dve.Fori(0, NB // 2) as pr:
                a0 = pr * 2
                for p in range(2):
                    dve.wait_ge(a2_stored[p], 24 * a0)
                    dve.wait_ge(gate_exp, a0 + p + 1)
                    v.tensor_tensor(ab_y[p], ab_bank[p][:, 0:4], dt_b[:, :], ALU.add)
                    dve.drain()
                    v.scalar_tensor_tensor(ab_e[p][:, 0:4], ab_y[p], -1.0, ab_y[p], ALU.mult, ALU.min).then_inc(ab_sum, 1)
                    one_over_one_plus(g_exp[p])
                    v.tensor_tensor(g_out[p], ag_bank[p], g_exp[p], ALU.mult).then_inc(gate_done, 1)
                    dve.wait_ge(ab_exp, a0 + p + 1)
                    v.scalar_tensor_tensor(ab_out[p][:, 0:4], ab_y[p], 0.0, ab_e[p][:, 0:4], ALU.max, ALU.add)
                    one_over_one_plus(ab_e[p][:, 4:8])
                    v.tensor_copy(ab_out[p][:, 4:8], ab_e[p][:, 4:8])
                    v.scalar_tensor_tensor(ab_out[p][:, 0:4], ab_out[p][:, 0:4], -1.0, a_neg[:, :], ALU.mult, ALU.mult).then_inc(ab_done, 1)

            dve.wait_ge(wout_landed, 16)
            for k in range(KC):
                col = R_OUT + k if k < 4 else R_GOUT
                last = v.tensor_scalar(w_out_sb[:, k, :], w_out_sb[:, k, :], vecs[:, col:col + 1], None, ALU.mult)
            last.then_inc(wout_scaled, 1)
            v.memset(g_sel, 0.0)
            dve.drain()

            def fill(i, g, u):
                if not u:
                    return
                for k in range(GS):
                    dve.wait_ge(u_landed[k], 16 * (NG * (i - 1) + g + 1))
                    v.scalar_tensor_tensor(u_ring[:, k, :], u_ring[:, k, :], 1.0, hn_cur, ALU.mult, ALU.mult,
                                           accum_out=dots[:, bass.ds(g * GS + k, 1)]).then_inc(dotted, 1)

            def mixing(b, i, u, loop):
                t0 = steps_before(b)
                beta = ab_in[:, GH:2 * GH]
                dve.wait_ge(gdn_landed, 96 * (b + 1))
                v.tensor_copy(g_sel[0:64, 0:4], ab_in[0:64, 0:4])
                v.tensor_copy(g_sel[64:128, 4:8], ab_in[64:128, 0:4]).then_inc(g_split, 1)
                if isinstance(b, int) and b == 0:
                    v.memset(state, 0.0)
                dve.wait_ge(g_summed, b + 1)
                v.tensor_copy(ex_in[:, 0:4], bank(ox, 1)[:, 0:4])
                v.tensor_copy(ex_in[:, 8:16], bank(ox, 1)[:, 4:12])
                dve.drain()
                v.tensor_tensor(ex_in[0:64, 4:8], ex_in[0:64, 8:12], ex_in[0:64, 0:4], ALU.subtract)
                v.tensor_tensor(ex_in[64:128, 4:8], ex_in[64:128, 12:16], ex_in[64:128, 0:4], ALU.subtract).then_inc(ex_ready, 1)
                v.tensor_tensor(heads(t_xt, 4), every(ident[:, :], 4), spread(ex_in[:, 0:4], 4, P), ALU.mult)
                v.tensor_tensor(heads(t_p, 4), every(ident[:, :], 4), spread(beta, 4, P), ALU.mult).then_inc(diags_ready, 1)
                dve.wait_ge(qd_exp, b + 1)
                v.tensor_tensor(heads(t_dt, 4), heads(bank(zz, 0), 4), spread(ex_in[:, 0:4], 4, P), ALU.subtract)
                dve.drain()
                v.tensor_scalar(t_dt, t_dt, 0.0, None, ALU.min).then_inc(decay_arg, 1)
                dve.wait_ge(ex_done, b + 1)
                v.tensor_tensor(kbg_w, beta, ex[:, 0:4], ALU.mult)
                v.tensor_tensor(heads(t_vb, 4), heads(gv, 4), spread(beta, 4, P), ALU.mult)
                v.tensor_tensor(heads(t_kd, 4), heads(gk, 4), spread(ex[:, 4:8], 4, P), ALU.mult)
                dve.drain()
                v.tensor_tensor(heads(t_kbg, 4), heads(gk, 4), spread(kbg_w, 4, P), ALU.mult)
                dve.wait_ge(decay_exp, b + 1)
                v.tensor_tensor(heads(t_dt, 4), heads(t_dt, 4), every(upto[:, :], 4), ALU.mult)
                v.tensor_tensor(t_qd, t_qd, gqT, ALU.mult)
                dve.drain()
                v.tensor_tensor(t_at, t_dt, bank(zz, 1), ALU.mult)
                dve.drain()
                dve.wait_ge(pairs_done, b + 1)
                v.tensor_tensor(t_at, t_at, bank(rr, 0), ALU.mult)
                v.tensor_tensor(t_dt, t_dt, bank(rr, 1), ALU.mult)
                dve.drain()
                v.tensor_tensor(heads(t_xt, 4), heads(t_at, 4), every(levels[:, 0, :], 4), ALU.mult)
                dve.drain()
                v.tensor_tensor(heads(t_TT, 4), every(ident[:, :], 4), heads(t_xt, 4), ALU.subtract).then_inc(tt_first, 1)
                fill(i, 0, u)
                for lv in range(1, 6):
                    dve.drain()
                    v.tensor_tensor(heads(t_xt, 4), heads(t_at, 4), every(levels[:, lv, :], 4), ALU.mult).then_inc(x_ready, 1)
                    dve.wait_ge(corr_done, 5 * b + lv)
                    if lv < 5:
                        v.tensor_tensor(t_T, t_T, bank(zz, 1), ALU.subtract)
                    v.tensor_tensor(t_TT, t_TT, bank(rr, 0), ALU.subtract).then_inc(t_ready, 1)
                    fill(i, lv, u)
                dve.wait_ge(uw_copied, b + 1)
                for c in range(2):
                    r = slice(64 * c, 64 * c + 64)
                    dve.wait_ge(ws_done, 2 * b + c + 1)
                    v.tensor_tensor(t_vn[r, :], t_u[r, :], bank(zz, 0)[r, :], ALU.subtract).then_inc(vn_ready, 1)
                    dve.drain()
                    dve.wait_ge(kv_done, 2 * b + c + 1)
                    for h in range(GH):
                        last = v.scalar_tensor_tensor(heads(state, 4)[:, h, :], heads(state, 4)[:, h, :],
                                                      ex[:, 8 + 4 * c + h:9 + 4 * c + h], heads(bank(zz, 1), 4)[:, h, :],
                                                      ALU.mult, ALU.add)
                    last.then_inc(state_ready, 1)
                    fill(i, 6 + c, u)

                def key_step(t, g, first=False):
                    for hg in range(2):
                        dve.wait_ge(l_done[hg], t + 1)
                        dve.wait_ge(rest_done[hg], t)
                        sp = v.scalar_tensor_tensor(att_sp[hg], bank(zz, hg), 0.0, att_l[hg], ALU.max, ALU.add)
                        if first:
                            dve.drain()
                            sp = v.tensor_tensor(heads(att_sp[hg], 4), heads(att_sp[hg], 4), every(visible[:, :], 4), ALU.mult)
                        sp.then_inc(sp_done[hg], 1)
                        dve.wait_ge(pv_done[hg], t)
                        v.scalar_tensor_tensor(att_u[hg], bank(zz, hg), 0.0, att_l[hg], ALU.min,
                                               ALU.subtract).then_inc(z_used[hg], 1)
                    fill(i, g, u)
                    for hg in range(2):
                        dve.drain()
                        dve.wait_ge(later_done[hg], t + 1)
                        arg = v.tensor_tensor(att_u[hg], att_u[hg], bank(rr, hg), ALU.subtract)
                        if first:
                            dve.drain()
                            arg = v.tensor_tensor(heads(att_u[hg], 4), heads(att_u[hg], 4), every(hidden[:, :], 4), ALU.add)
                        arg.then_inc(arg_done[hg], 1)

                key_step(t0, 8, first=True)
                loop(dve, b, lambda t: key_step(t0 + t, 8 + t))
                dve.wait_ge(o_squared, b + 1)
                v.tensor_reduce(ss12[:, 0:8], heads(sq_att, SBH), AX.X, ALU.add)
                v.tensor_reduce(ss12[:, 8:12], heads(sq_gdn, GH), AX.X, ALU.add)
                dve.drain()
                v.tensor_scalar(ms12[:, 0:8], ss12[:, 0:8], 1.0 / SBD, EPS, ALU.mult, ALU.add)
                v.tensor_scalar(ms12[:, 8:12], ss12[:, 8:12], 1.0 / GD, EPS, ALU.mult, ALU.add).then_inc(o_meaned, 1)
                dve.wait_ge(o_seeded, b + 1)
                newton(r12, y12, ms12, a12)
                v.tensor_scalar(r12, r12, -0.5, None, ALU.mult)
                dve.drain()
                v.tensor_tensor(heads(mix[:, 512:1024], GH), heads(mix[:, 512:1024], GH), spread(r12[:, 8:12], GH, GD), ALU.mult)
                v.tensor_tensor(heads(mix[:, 0:512], SBH), heads(bank(ox, 0), SBH), spread(r12[:, 0:8], SBH, SBD), ALU.mult)
                dve.drain()
                v.tensor_tensor(mix[:, 512:1024], mix[:, 512:1024], gate, ALU.mult).then_inc(mix_done, 1)
                g = 9 + b
                fill(i, g, u)
                dve.wait_ge(mix_turned, b + 1)
                v.tensor_copy(mixT[:, 512:1024], bank(rr, 1)).then_inc(mixT_dve, 1)
                fill(i, g + 1, u)
                dve.wait_ge(xb_landed, 16 * (b + 1))
                dve.wait_ge(out_done, b + 1)
                v.tensor_tensor(h_sb, zz[:, :], x_in, ALU.add).then_inc(h_done, 1)
                dve.wait_ge(h_squared, b + 1)
                v.tensor_scalar(msh, ssh, 1.0 / D, EPS, ALU.mult, ALU.add).then_inc(h_meaned, 1)
                dve.wait_ge(h_seeded, b + 1)
                newton(rh, yh, msh, ah)
                v.tensor_scalar(rh, rh, -0.5, None, ALU.mult)
                dve.drain()
                v.scalar_tensor_tensor(hn_new, h_sb, rh, norm2b[:, :], ALU.mult, ALU.mult).then_inc(hn_done, 1)
                fill(i, g + 2, u)
                dve.wait_ge(hn_turned, b + 1)
                v.tensor_copy(hnT[:, 512:1024], bank(rr, 1)).then_inc(hnT_dve, 1)
                for q in range(4):
                    fill(i, g + 3 + q, u)
                for q in range(4):
                    four = [(h, c) for h in (2 * q, 2 * q + 1) for c in range(2)]
                    count = settled(dve, 4 * b + q + 1)
                    known(dve)
                    dve.wait_ge(sc_copied, count)
                    for h, c in four:
                        v.max(top_v[:, h, c, 0:8], sc[:, h, c, :])
                    dve.drain()
                    for h, c in four:
                        v.max_index(top_i[:, h, c, 0:8], top_v[:, h, c, 0:8], sc[:, h, c, :])
                    dve.drain()
                    for h, c in four:
                        v.match_replace(sc[:, h, c, :], top_v[:, h, c, 0:8], sc[:, h, c, :], -BIG)
                    dve.drain()
                    for h, c in four:
                        v.max(top_v[:, h, c, 8:16], sc[:, h, c, :])
                    dve.drain()
                    for h, c in four:
                        v.max_index(top_i[:, h, c, 8:16], top_v[:, h, c, 8:16], sc[:, h, c, :])
                    fill(i, g + 7 + q, u)
                dve.drain()
                v.tensor_tensor(cand, top_v[:, :, 0, :].unsqueeze(3).to_broadcast([P, PH, TOPK, TOPK]),
                                top_v[:, :, 1, :].unsqueeze(2).to_broadcast([P, PH, TOPK, TOPK]), ALU.add)
                v.tensor_copy(top_f, top_i)
                dve.drain()
                flat = T(W + 4, 4).rearrange("p (h n) -> p h n", h=PH)
                for q in range(2):
                    hs = range(4 * q, 4 * q + 4)
                    for h in hs:
                        v.max(best[:, h, 0:8], flat[:, h, :])
                    dve.drain()
                    for h in hs:
                        v.max_index(ci[:, h, 0:8], best[:, h, 0:8], flat[:, h, :])
                    dve.drain()
                    for h in hs:
                        v.match_replace(flat[:, h, :], best[:, h, 0:8], flat[:, h, :], -BIG)
                    dve.drain()
                    for h in hs:
                        v.max(best[:, h, 8:16], flat[:, h, :])
                    dve.drain()
                    for h in hs:
                        v.max_index(ci[:, h, 8:16], best[:, h, 8:16], flat[:, h, :])
                    fill(i, g + 11 + q, u)
                dve.drain()
                v.tensor_copy(gsum, best[:, :, 0])
                ci_flat = small[:, 896:1024].bitcast(U32)
                v.tensor_scalar(ci_hi, ci_flat, 4, None, ALU.logical_shift_right)
                dve.drain()
                v.tensor_tensor(best, best, spread(gsum, PH, TOPK), ALU.subtract).then_inc(best_shifted, 1)
                for table, which, e in ((0, ci_hi, e1), (1, ci_flat, e2)):
                    if table:
                        dve.drain()
                        v.tensor_scalar(ci_flat, ci_flat, TOPK - 1, None, ALU.bitwise_and)
                        dve.drain()
                    v.tensor_copy(ci_f, which.rearrange("p (h k) -> p h k", h=PH))
                    dve.drain()
                    v.tensor_tensor(hot, ci_f.unsqueeze(3).to_broadcast([P, PH, TOPK, TOPK]),
                                    iota16[:, :].unsqueeze(1).unsqueeze(1).to_broadcast([P, PH, TOPK, TOPK]), ALU.is_equal)
                    dve.drain()
                    v.tensor_tensor(hot, hot, top_f[:, :, table, :].unsqueeze(2).to_broadcast([P, PH, TOPK, TOPK]), ALU.mult)
                    dve.drain()
                    v.tensor_reduce(e, hot, AX.X, ALU.add)
                fill(i, g + 13, u)
                dve.wait_ge(best_exp, b + 1)
                v.tensor_reduce(gsum, best, AX.X, ALU.add)
                dve.drain()
                v.reciprocal(gsum, gsum)
                dve.drain()
                v.tensor_tensor(gate_new[:, :].rearrange("p (h k) -> p h k", h=PH), best, spread(gsum, PH, TOPK), ALU.mult)
                dve.wait_ge(idx_moved, i)
                v.scalar_tensor_tensor(idx_new[:, :].rearrange("p (h k) -> p h k", h=PH), e1, float(NK), e2,
                                       ALU.mult, ALU.add).then_inc(topk_done, 1)
                return g + 14

            def ending(i, m, u, w):
                dve.drain()
                if u:
                    v.tensor_tensor(gelu_t[:, :], dots[:, :], dots[:, :], ALU.mult)
                    dve.drain()
                    v.tensor_scalar(gelu_t[:, :], gelu_t[:, :], GELU_C, 1.0, ALU.mult, ALU.add)
                    dve.drain()
                    v.tensor_tensor(gelu_t[:, :], gelu_t[:, :], dots[:, :], ALU.mult)
                    dve.drain()
                    v.tensor_scalar(gelu_t[:, :], gelu_t[:, :], -50.0, None, ALU.max).then_inc(gelu_arg, 1)
                    dve.wait_ge(gelu_exp, i)
                    one_over_one_plus(gelu_t[:, :])
                    v.tensor_tensor(gelu_t[:, :], gelu_t[:, :], dots[:, :], ALU.mult)
                    dve.drain()
                    if w:
                        dve.wait_ge(diag_done, SLOTS * (i - 1))
                    v.tensor_tensor(act_w[:, :], gelu_t[:, :], gate_cur[:, :], ALU.mult).then_inc(act_done, 1)
                    dve.drain()
                if m:
                    v.tensor_copy(gate_cur[:, :], gate_new[:, :])
                    v.tensor_copy(hn_cur, hn_new)
                    dve.drain()
                if w:
                    dve.wait_ge(h_back, 16 * (i - 1))
                    dve.wait_ge(v_used, GS + SLOTS * (i - 1))
                    v.tensor_tensor(y_buf, va[:, :], y_buf, ALU.add).then_inc(y_done, 1)

            def rest_groups(i, g, u):
                with dve.Fori(g, NG) as gg:
                    fill(i, gg, u)

            def py_loop(e, b, body):
                for t in range(1, b + 1):
                    body(t)

            def fori_loop(e, b, body):
                with e.Fori(1, b + 1) as t:
                    body(t)

            mixing(0, 0, False, py_loop)
            ending(0, True, False, False)
            g = mixing(1, 1, True, py_loop)
            rest_groups(1, g, True)
            ending(1, True, True, False)
            with dve.Fori(2, NB) as i:
                g = mixing(i, i, True, fori_loop)
                rest_groups(i, g, True)
                ending(i, True, True, True)
            rest_groups(NB, 0, True)
            ending(NB, False, True, True)
            ending(NB + 1, False, False, True)

        @block.tensor
        def _(pe):
            t_ = nc.tensor

            def mm(out_, lhsT, rhs, start=True, stop=True):
                return t_.matmul(out_, lhsT, rhs, start=start, stop=stop, skip_group_check=True)

            def turn(dst, src, n):
                for c in range(n):
                    last = t_.transpose(dst[:, c * P:(c + 1) * P], src[:, c * P:(c + 1) * P], ident[:, :])
                return last

            pe.wait_ge(consts, 1)
            t_.nop().then_inc(v_used, GS)
            for n in range(NB):
                pe.wait_ge(x_scaled, n + 1)
                if n >= 2:
                    pe.wait_ge(xT_act, n - 1)
                    pe.wait_ge(xT_dve, n - 1)
                turn((zz if n % 2 == 0 else rr)[:, :], x_all[:, n, :], KC).then_inc(x_turned, 1)
            pe.wait_ge(consts_loaded, 16 * len(vec_loads))
            turn(bank(va, 1), vec_rows, 1).then_inc(vec_turned, 1)
            for n in range(2):
                pe.wait_ge(sub_landed, 16 * (n + 1))
                if n:
                    pe.wait_ge(sub_copied, 1)
                turn(ox[:, :], work[:, 16384:17408], PH).then_inc(sub_turned, 1)
            pe.wait_ge(w_in_scaled, KC // 2)
            pe.wait_ge(w_in_scaled_act, KC // 2)
            pe.wait_ge(xT_act, NB)
            pe.wait_ge(xT_dve, NB)
            pe.wait_ge(sub_copied, 2)
            with pe.Fori(0, 2) as half:
                for n in range(NCH + 8):
                    if n < NCH:
                        col = CH[n][2]
                        pe.wait_ge(evacuated, NCH * half + (n - 1 if n >= 2 else 0))
                        for k in range(KC):
                            last = mm(mm_bank[n % 2], w_in_sb[:, k, col:col + P], xT[:, k, bass.ds(half * HALF, HALF)],
                                      k == 0, k == KC - 1)
                        last.then_inc(projected, 1)
                    m = n - 3
                    if 0 <= m < NCH and CH[m][0] != "v":
                        c = norm_count(m) - 1
                        pe.wait_ge(normed, NCH * half + (m - 2 if c >= 3 else 0))
                        pe.wait_ge(squared, 16 * half + c + 1)
                        mm(ss_bank[c % 3], (ones if CH[m][0] == "g" else mean64)[:, :], sq_ring[c % 2]).then_inc(summed, 1)
                    m = n - 6
                    if 0 <= m < NCH and needs_tokens(m):
                        t = token_count(m) - 1
                        pe.wait_ge(normed, NCH * half + m + 1)
                        pe.wait_ge(turned_copied, 8 * half + (t - 1 if t >= 2 else 0))
                        turn(tr_bank[t % 2], o_ring[m % 4], 4).then_inc(turned, 1)
            pe.wait_ge(normed, 2 * NCH)
            pe.wait_ge(turned_copied, 16)
            with pe.Fori(0, NB // 2) as pr:
                a0 = pr * 2
                pe.wait_ge(v_copied, a0)
                pe.wait_ge(gate_done, a0)
                pe.wait_ge(ab_done, a0)
                for p in range(2):
                    pe.wait_ge(x_staged, a0 + p + 1)
                    for bk, c0, n in ((av_bank[p], COL_SV, SBW), (ag_bank[p], COL_GATE, GW), (ab_bank[p], COL_AB, 2 * GH)):
                        for k in range(KC):
                            last = mm(bk, stage_x[p][:, k, :], w_in_sb[:, k, c0:c0 + n], k == 0, k == KC - 1)
                    last.then_inc(tok_projected, 1)

            def fill(i, g, v, first=False, last_one=False):
                if not v:
                    return
                for k in range(GS):
                    pe.wait_ge(v_landed[k], 16 * (NG * (i - 2) + g + 1))
                    pe.wait_ge(diag_done, GS * (NG * (i - 2) + g) + k + 1)
                    st, sp = first and k == 0, last_one and k == GS - 1
                    mm(bank(va, 0), diag[:, k, :], v_ring[:, k, 0:512], st, sp)
                    mm(bank(va, 1), diag[:, k, :], v_ring[:, k, 512:1024], st, sp).then_inc(v_used, 1)

            def four(dst, lhs, rhs):
                for h in range(GH):
                    last = mm(heads(dst, 4)[:, h, :], heads(lhs, 4)[:, h, :], heads(rhs, 4)[:, h, :])
                return last

            def mixing(b, i, v, loop):
                t0 = steps_before(b)
                pe.wait_ge(g_split, b + 1)
                mm(bank(ox, 1)[:, 0:4], upto[:, :], ab_in[:, 0:4])
                mm(bank(ox, 1)[:, 4:12], ones[:, :], g_sel).then_inc(g_summed, 1)
                pe.wait_ge(diags_ready, b + 1)
                mm(bank(zz, 0), ones[:, :], t_xt)
                mm(bank(zz, 1), ones[:, :], t_p).then_inc(spread_done, 1)
                four(bank(rr, 0), gkT, gkT)
                four(bank(rr, 1), gkT, gqT).then_inc(pairs_done, 1)
                pe.wait_ge(tt_first, b + 1)
                turn(bank(ox, 1), t_TT, 4).then_inc(tt_turned, 1)
                if v:
                    if not isinstance(i, int) or i > 2:
                        pe.wait_ge(y_done, i - 2)
                fill(i, 0, v, first=True)
                for lv in range(1, 6):
                    pe.wait_ge(x_ready, 5 * b + lv)
                    if lv == 1:
                        pe.wait_ge(tt_copied, b + 1)
                    else:
                        pe.wait_ge(t_ready, 5 * b + lv - 1)
                    four(bank(zz, 0), t_xt, t_T).then_inc(p_done, 1)
                    pe.wait_ge(p_copied, 5 * b + lv)
                    if lv < 5:
                        four(bank(zz, 1), t_TT, t_p)
                    four(bank(rr, 0), t_p, t_TT).then_inc(corr_done, 1)
                    fill(i, lv, v)
                pe.wait_ge(t_ready, 5 * b + 5)
                four(bank(rr, 1), t_TT, t_vb)
                four(bank(ox, 1), t_kbg, t_TT).then_inc(uw_done, 1)
                og = bank(ox, 0)
                pe.wait_ge(uw_copied, b + 1)
                for c in range(2):
                    r = slice(64 * c, 64 * c + 64)
                    if c:
                        pe.wait_ge(state_ready, 2 * b + 1)
                    for h in range(GH):
                        last = mm(heads(bank(zz, 0), 4)[r, h, :], heads(t_wT, 4)[:, h, r], heads(state, 4)[:, h, :])
                    last.then_inc(ws_done, 1)
                    for h in range(GH):
                        mm(heads(og, 4)[r, h, :], heads(t_qd, 4)[:, h, r], heads(state, 4)[:, h, :], h == 0, False)
                    pe.wait_ge(vn_ready, 2 * b + c + 1)
                    for h in range(GH):
                        last = mm(heads(bank(zz, 1), 4)[:, h, :], heads(t_kd, 4)[r, h, :], heads(t_vn, 4)[r, h, :])
                    last.then_inc(kv_done, 1)
                    fill(i, 6 + c, v)
                for h in range(GH):
                    last = mm(heads(og, 4)[:, h, :], heads(t_dt, 4)[:, h, :], heads(t_vn, 4)[:, h, :], False, h == GH - 1)
                last.then_inc(og_done, 1)
                pe.wait_ge(state_ready, 2 * b + 2)
                pe.wait_ge(og_copied, b + 1)

                def key_step(t, g, first=False):
                    if first:
                        pe.wait_ge(q_landed, 16 * (b + 1))
                    pe.wait_ge(k_landed, 16 * (t + 1))
                    for hg in range(2):
                        pe.wait_ge(z_used[hg], t)
                        r = slice(64 * hg, 64 * hg + 64)
                        for h in range(4):
                            last = mm(heads(bank(zz, hg), 4)[:, h, :], heads(kTj, 4)[r, h, :], heads(qT, 4)[r, h, :])
                        last.then_inc(z_done[hg], 1)
                    fill(i, g, v)
                    for hg in range(2):
                        pe.wait_ge(sp_done[hg], t + 1)
                        mm(bank(rr, hg), later[:, :], att_sp[hg], first, True).then_inc(later_done[hg], 1)
                    for hg in range(2):
                        pe.wait_ge(arg_done[hg], t + 1)
                        mm(bank(rr, hg), rest[:, :], att_sp[hg], False, True).then_inc(rest_done[hg], 1)
                    for hg in range(2):
                        pe.wait_ge(vj_landed, 16 * (t + 1))
                        pe.wait_ge(w_done[hg], t + 1)
                        for h in range(4):
                            c = (2 * h + hg) * SBD
                            last = mm(bank(ox, 0)[:, c:c + SBD], heads(att_u[hg], 4)[:, h, :], vj[:, c:c + SBD],
                                      first and hg == 0 and h == 0, False)
                        last.then_inc(pv_done[hg], 1)

                key_step(t0, 8, first=True)
                loop(pe, b, lambda t: key_step(t0 + t, 8 + t))
                g = 9 + b
                pe.wait_ge(mix_done, b + 1)
                turn(rr[:, :], mix, KC).then_inc(mix_turned, 1)
                fill(i, g, v)
                pe.wait_ge(mixT_act, b + 1)
                pe.wait_ge(mixT_dve, b + 1)
                if isinstance(b, int) and b == 0:
                    pe.wait_ge(wout_scaled, 1)
                    pe.wait_ge(wq_landed, 16)
                for n in range(2):
                    for k in range(KC):
                        last = mm(bank(zz, n), mixT[:, k * P:(k + 1) * P], w_out_sb[:, k, n * HALF:(n + 1) * HALF],
                                  k == 0, k == KC - 1)
                last.then_inc(out_done, 1)
                fill(i, g + 1, v)
                pe.wait_ge(hn_done, b + 1)
                turn(rr[:, :], hn_new, KC).then_inc(hn_turned, 1)
                fill(i, g + 2, v)
                pe.wait_ge(hnT_act, b + 1)
                pe.wait_ge(hnT_dve, b + 1)
                pair = (zz, rr)
                for q in range(4):
                    for c in range(4):
                        col = (4 * q + c) * P
                        for k in range(KC):
                            last = mm(heads(bank(pair[q // 2], q % 2), 4)[:, c, :], w_q_sb[:, k, col:col + P],
                                      hnT[:, k * P:(k + 1) * P], k == 0, k == KC - 1)
                    last.then_inc(pq_done, 1)
                    fill(i, g + 3 + q, v)
                pe.wait_ge(sub_in_b, 16 * (b + 1))
                for q in range(4):
                    pe.wait_ge(pq_copied, 4 * b + q + 1)
                    for c in range(4):
                        last = mm(heads(bank(pair[q // 2], q % 2), 4)[:, c, :], pqT[:, 4 * q + c, :], subT[:, 4 * q + c, :])
                    last.then_inc(sc_done, 1)
                for q in range(7):
                    fill(i, g + 7 + q, v)
                pe.wait_ge(sc_copied, 4 * b + 4)
                return g + 14

            def rest_groups(i, g):
                if isinstance(g, int) and g == 0:
                    pe.wait_ge(y_done, i - 2)
                    fill(i, 0, True, first=True)
                    g = 1
                with pe.Fori(g, NG - 1) as gg:
                    fill(i, gg, True)
                fill(i, NG - 1, True, last_one=True)

            def py_loop(e, b, body):
                for t in range(1, b + 1):
                    body(t)

            def fori_loop(e, b, body):
                with e.Fori(1, b + 1) as t:
                    body(t)

            mixing(0, 0, False, py_loop)
            mixing(1, 1, False, py_loop)
            with pe.Fori(2, NB) as i:
                rest_groups(i, mixing(i, i, True, fori_loop))
            rest_groups(NB, 0)
            rest_groups(NB + 1, 0)


_INS = ["x", "norm1_w", "w_in", "sb_q_norm_w", "sb_k_norm_w", "sb_out_norm_w", "gdn_conv_w", "gdn_a_log",
        "gdn_dt_bias", "gdn_out_norm_w", "w_out", "norm2_w", "peer_w_q", "peer_sub_keys_1", "peer_sub_keys_2",
        "peer_u", "peer_v"]


def kernel(**inputs):
    import concourse.bacc as bacc
    import numpy as np
    from concourse.bass_utils import run_bass_kernel_spmd

    nc = bacc.Bacc("TRN2", target_bir_lowering=False, num_devices=1)
    arrays, args = {}, []
    for name in _INS:
        a = np.ascontiguousarray(inputs[name])
        arrays[f"in_{name}"] = a
        args.append(nc.dram_tensor(f"in_{name}", a.shape, mybir.dt.from_np(a.dtype), kind="ExternalInput").ap())
    out = nc.dram_tensor("out_y", (1, S, D), F32, kind="ExternalOutput").ap()
    hybrid_layer_kernel(nc, *args, out)
    r = run_bass_kernel_spmd(nc, [arrays], core_ids=[0])
    return r.results[0]["out_y"]
```

```python
import math
from contextlib import ExitStack

import concourse.bass as bass
from concourse import mybir

F32 = mybir.dt.float32
BF16 = mybir.dt.bfloat16
U32 = mybir.dt.uint32
ALU = mybir.AluOpType
ACT = mybir.ActivationFunctionType
AX = mybir.AxisListType

P = 128
S, D = 1024, 1024
NB = S // P
KC = D // P
SBH, SBD = 8, 64
GH, GD = 4, 128
CHUNK = 64
TAPS = 4
SBW, GW = SBH * SBD, GH * GD
COL_SV = 2 * SBW
COL_G = 3 * SBW
COL_GATE = COL_G + 3 * GW
COL_AB = COL_GATE + GW
INC = COL_AB + 2 * GH
PH, NK, TOPK = 8, 128, 16
SLOTS = PH * TOPK
GS = 4
NG = SLOTS // GS
EPS = 1e-6
HALF = 512
NEG = -1e30
BIG = 3e38
GELU_C = 0.044715
GELU_S = math.sqrt(2.0 / math.pi)

_COLS = {"g": COL_G, "v": COL_G + 8 * P, "s": 0}
CH = []
for _kind in "gsvgs" * 3 + "gvgss":
    _c = sum(k == _kind for k, _, _ in CH)
    CH.append((_kind, _c, _COLS[_kind] + _c * P))
NCH = len(CH)
ACT_CHUNKS = (0, 3, 5)


def conv_count(n):
    return sum(k in "gv" for k, _, _ in CH[:n + 1])


def norm_count(n):
    return sum(k in "gs" for k, _, _ in CH[:n + 1])


def needs_tokens(n):
    return CH[n][0] == "v" or (CH[n][0] == "g" and CH[n][1] >= GH)


def stores_before(n, slot):
    return sum(k != "v" for k, _, _ in CH[slot:n:4])


def token_count(n):
    return sum(needs_tokens(m) for m in range(n + 1))


def hybrid_layer_kernel(nc, x, norm1_w, w_in, sb_q_norm_w, sb_k_norm_w, sb_out_norm_w, gdn_conv_w,
                        gdn_a_log, gdn_dt_bias, gdn_out_norm_w, w_out, norm2_w, peer_w_q,
                        peer_sub_keys_1, peer_sub_keys_2, peer_u, peer_v, out):
    x_blk = x[0].rearrange("(n p) d -> n p d", p=P)
    out_blk = out[0].rearrange("(n p) d -> n p d", p=P)
    u_rows, v_rows = peer_u[0], peer_v[0]

    def scratch(name, shape):
        return nc.dram_tensor(name, shape, F32, kind="Internal").ap()

    d_qT = scratch("d_qT", (NB, P, 4, P))
    d_kT = scratch("d_kT", (NB, P, 4, P))
    d_v = scratch("d_v", (NB, P, SBW))
    d_gqT = scratch("d_gqT", (NB, P, GH, P))
    d_gkT = scratch("d_gkT", (NB, P, GH, P))
    d_gk = scratch("d_gk", (NB, P, GH, P))
    d_gv = scratch("d_gv", (NB, P, GH, P))
    d_gate = scratch("d_gate", (NB, P, GW))
    d_ab = scratch("d_ab", (NB, P, 2 * GH))
    d_subT = scratch("d_subT", (P, 2 * PH, NK))
    d_h = scratch("d_h", (NB, P, D))

    ctx = ExitStack()
    with ctx:
        def sb(name, shape, dt=F32):
            return ctx.enter_context(nc.sbuf_tensor(name, shape, dt))

        def sem(name):
            return ctx.enter_context(nc.semaphore(name))

        ident = sb("ident", [P, P])
        ones = sb("ones", [P, P])
        later = sb("later", [P, P])
        rest = sb("rest", [P, P])
        visible = sb("visible", [P, P], BF16)
        hidden = sb("hidden", [P, P], BF16)
        mean64 = sb("mean64", [P, P])
        upto = sb("upto", [P, P])
        levels = sb("levels", [P, 6, P], BF16)
        iota16 = sb("iota16", [P, TOPK])
        vecs = sb("vecs", [P, P])
        norm2b = sb("norm2b", [P, D])
        a_neg = sb("a_neg", [P, GH])
        dt_b = sb("dt_b", [P, GH])
        weights = sb("weights", [P, KC * INC])
        work = sb("work", [P, 20160])

        dots = sb("dots", [P, SLOTS])
        act_w = sb("act_w", [P, SLOTS])
        gate_cur = sb("gate_cur", [P, SLOTS])
        gate_new = sb("gate_new", [P, SLOTS])
        idx_new = sb("idx_new", [P, SLOTS], U32)
        idx_u = sb("idx_u", [P, SLOTS], U32)
        idx_v = sb("idx_v", [P, SLOTS], U32)
        stage_u = [sb(f"stage_u{p}", [P, GS], U32) for p in range(2)]
        stage_v = [sb(f"stage_v{p}", [P, GS], U32) for p in range(2)]
        gelu_t = sb("gelu_t", [P, SLOTS])
        diag = sb("diag", [P, GS, P])
        ab_in = sb("ab_in", [P, 2 * GH])
        sm = sb("sm", [P, 192])

        zz = ctx.enter_context(nc.psum_tensor("zz", [P, 2 * HALF], F32))
        rr = ctx.enter_context(nc.psum_tensor("rr", [P, 2 * HALF], F32))
        ox = ctx.enter_context(nc.psum_tensor("ox", [P, 2 * HALF], F32))
        va = ctx.enter_context(nc.psum_tensor("va", [P, 2 * HALF], F32))

        def bank(t, n):
            return t[:, n * HALF:(n + 1) * HALF]

        w_in_sb = weights[:, :].rearrange("p (k n) -> p k n", k=KC)
        xT = work[:, 0:KC * S].rearrange("p (k t) -> p k t", k=KC)
        x_all = work[:, 8192:8192 + NB * D].rearrange("p (n d) -> p n d", n=NB)
        sub_at = [work[:, n:n + PH * NK] for n in (16384, 18560, 17408)]
        sub_in = sub_at[0:2]
        sub_out = [sub_at[2], sub_at[0]]
        vec_rows = work[:, 18432:18560]
        A0 = 8192

        def tile_a(n):
            return work[:, A0 + n * 512:A0 + (n + 1) * 512]

        s_ring = [tile_a(n) for n in range(6)]
        e_ring = [tile_a(6 + n) for n in range(2)]
        sq_ring = [tile_a(8 + n) for n in range(2)]
        y_ring = [tile_a(10 + n) for n in range(2)]
        o_ring = [tile_a(12 + n) for n in range(4)]
        tok_ring = [tile_a(16 + n) for n in range(2)]
        tmp_a = [tile_a(18), tile_a(19)]
        cb = [work[:, A0 + 10240 + n * 516:A0 + 10240 + n * 516 + 515] for n in range(2)]
        hist = work[:, A0 + 11280:A0 + 11280 + 36].rearrange("p (c k) -> p c k", c=12)
        mm_bank = [bank(zz, 0), bank(zz, 1)]
        ss_bank = [bank(rr, 0), bank(rr, 1), bank(ox, 0)]
        tr_bank = [bank(ox, 1), bank(va, 0)]
        stage_x = [work[:, A0 + n * 1024:A0 + (n + 1) * 1024].rearrange("p (k t) -> p k t", k=KC) for n in range(2)]
        v_out = [tile_a(4 + n) for n in range(2)]
        g_out = [tile_a(6 + n) for n in range(2)]
        g_exp = [tile_a(8 + n) for n in range(2)]
        ab_out = [work[:, A0 + 5120 + 16 * n:A0 + 5120 + 16 * n + 8] for n in range(2)]
        ab_y = [work[:, A0 + 5160 + 16 * n:A0 + 5160 + 16 * n + 4] for n in range(2)]
        ab_e = [work[:, A0 + 5200 + 16 * n:A0 + 5200 + 16 * n + 8] for n in range(2)]
        av_bank = [bank(zz, 0), bank(zz, 1)]
        ag_bank = [bank(rr, 0), bank(rr, 1)]
        ab_bank = [bank(ox, 0)[:, 0:8], bank(ox, 1)[:, 0:8]]

        w_q_sb = weights[:, 0:KC * 2048].rearrange("p (k n) -> p k n", k=KC)
        w_out_sb = weights[:, 16384:16384 + KC * D].rearrange("p (k n) -> p k n", k=KC)
        u_ring = weights[:, 24576:24576 + GS * D].rearrange("p (s d) -> p s d", s=GS)
        v_ring = work[:, 13824:13824 + GS * D].rearrange("p (s d) -> p s d", s=GS)
        hn_cur = work[:, 17920:17920 + D]
        y_buf = work[:, 18944:18944 + D]

        def T(n, m=1):
            return work[:, n * 512:(n + m) * 512]

        def heads(ap, h):
            return ap.rearrange("p (h c) -> p h c", h=h)

        gqT, gkT, gk, gv, gate = (T(n) for n in range(5))
        subT = heads(T(0, 4), 2 * PH)
        qT, kTj, vj = T(5), T(6), T(7)
        x_in = T(5, 2)
        W = 8
        t_xt, t_p = T(W), T(W + 1)
        t_dt, t_at, t_qd, t_vb, t_kbg, t_kd = (T(W + n) for n in range(2, 8))
        t_T, t_TT, t_u, t_wT, t_vn = (T(W + n) for n in range(8, 13))
        att_l, att_sp, att_u = [T(W), T(W + 3)], [T(W + 1), T(W + 4)], [T(W + 2), T(W + 5)]
        sq_att, sq_gdn = T(W + 6), T(W + 7)
        mixT = T(W, 2)
        h_sb = T(W + 2, 2)
        sq_h = T(W + 4, 2)
        hnT = T(W + 6, 2)
        pqT = heads(T(W + 8, 4), 2 * PH)
        sc = T(W, 4).rearrange("p (h c k) -> p h c k", h=PH, c=2)
        cand = T(W + 4, 4).rearrange("p (h i j) -> p h i j", h=PH, i=TOPK)
        hot = T(W + 8, 4).rearrange("p (h k j) -> p h k j", h=PH, k=TOPK)
        state = T(21)
        mix = T(22, 2)
        hn_new = mix
        small = work[:, 24 * 512:27 * 512]
        top_v = small[:, 0:256].rearrange("p (h c k) -> p h c k", h=PH, c=2)
        top_i = small[:, 256:512].bitcast(U32).rearrange("p (h c k) -> p h c k", h=PH, c=2)
        top_f = small[:, 512:768].rearrange("p (h c k) -> p h c k", h=PH, c=2)
        best = small[:, 768:896].rearrange("p (h k) -> p h k", h=PH)
        ci = small[:, 896:1024].bitcast(U32).rearrange("p (h k) -> p h k", h=PH)
        ci_hi = small[:, 1024:1152].bitcast(U32)
        ci_f = small[:, 1152:1280].rearrange("p (h k) -> p h k", h=PH)
        e1 = small[:, 1280:1408].rearrange("p (h k) -> p h k", h=PH)
        e2 = small[:, 1408:1536].rearrange("p (h k) -> p h k", h=PH)

        g_sel = sm[:, 0:8]
        ex_in = sm[:, 8:24]
        ex = sm[:, 24:40]
        kbg_w = sm[:, 40:44]
        ss12, ms12, y12, a12, r12 = (sm[:, 48 + 12 * n:60 + 12 * n] for n in range(5))
        ssh, msh, yh, ah, rh = (sm[:, 112 + n:113 + n] for n in range(5))
        ss8, ms8, y8, a8, r8 = (sm[:, 120 + 8 * n:128 + 8 * n] for n in range(5))
        gsum = sm[:, 160:168]

        consts = sem("consts")
        mask_step = sem("mask_step")
        consts_loaded = sem("consts_loaded")
        vec_clear, vec_turned, vecs_ready = sem("vec_clear"), sem("vec_turned"), sem("vecs_ready")
        vec_consts = sem("vec_consts")
        w_in_landed = [sem(f"w_in_landed{k}") for k in range(KC)]
        w_in_scaled = sem("w_in_scaled")
        w_in_scaled_act = sem("w_in_scaled_act")
        x_landed = [sem(f"x_landed{n}") for n in range(2)]
        x_squared, x_meaned, x_seeded, x_scaled = sem("x_squared"), sem("x_meaned"), sem("x_seeded"), sem("x_scaled")
        x_turned, xT_act, xT_dve = sem("x_turned"), sem("xT_act"), sem("xT_dve")
        sub_landed, sub_turned, sub_copied, sub_stored = ([sem("sub_landed0"), sem("sub_landed1")], sem("sub_turned"),
                                                          sem("sub_copied"), sem("sub_stored"))
        projected, evacuated, convolved, exp_done = sem("projected"), sem("evacuated"), sem("convolved"), sem("exp_done")
        silu_done, squared, summed, seeded, normed = (sem("silu_done"), sem("squared"), sem("summed"),
                                                      sem("seeded"), sem("normed"))
        turned, turned_copied = sem("turned"), sem("turned_copied")
        o_stored = [sem(f"o_stored{n}") for n in range(4)]
        tok_stored = [sem(f"tok_stored{n}") for n in range(2)]
        x_staged, tok_projected = sem("x_staged"), sem("tok_projected")
        v_copied, gate_exp, gate_done, ab_sum, ab_exp, ab_done = (sem("v_copied"), sem("gate_exp"), sem("gate_done"),
                                                                   sem("ab_sum"), sem("ab_exp"), sem("ab_done"))
        a2_stored = [sem(f"a2_stored{n}") for n in range(2)]
        wq_landed, wout_landed, wout_scaled = sem("wq_landed"), sem("wout_landed"), sem("wout_scaled")
        gdn_landed = sem("gdn_landed")
        g_split, g_summed, ex_ready, ex_done = sem("g_split"), sem("g_summed"), sem("ex_ready"), sem("ex_done")
        diags_ready, spread_done, decay_arg, decay_exp = (sem("diags_ready"), sem("spread_done"),
                                                          sem("decay_arg"), sem("decay_exp"))
        qd_exp = sem("qd_exp")
        pairs_done, tt_first = sem("pairs_done"), sem("tt_first")
        x_ready, p_done, p_copied, corr_done, t_ready = (sem("x_ready"), sem("p_done"), sem("p_copied"),
                                                         sem("corr_done"), sem("t_ready"))
        tt_turned, tt_copied = sem("tt_turned"), sem("tt_copied")
        uw_done, uw_copied = sem("uw_done"), sem("uw_copied")
        ws_done, vn_ready, kv_done, state_ready = sem("ws_done"), sem("vn_ready"), sem("kv_done"), sem("state_ready")
        og_done, og_copied = sem("og_done"), sem("og_copied")

        q_landed = sem("q_landed")
        k_landed, vj_landed = sem("k_landed"), sem("vj_landed")
        z_done = [sem("z_done0"), sem("z_done1")]
        l_done = [sem("l_done0"), sem("l_done1")]
        sp_done = [sem("sp_done0"), sem("sp_done1")]
        z_used = [sem("z_used0"), sem("z_used1")]
        later_done = [sem("later_done0"), sem("later_done1")]
        arg_done = [sem("arg_done0"), sem("arg_done1")]
        rest_done = [sem("rest_done0"), sem("rest_done1")]
        w_done = [sem("w_done0"), sem("w_done1")]
        pv_done = [sem("pv_done0"), sem("pv_done1")]

        o_squared, o_meaned, o_seeded, mix_done = sem("o_squared"), sem("o_meaned"), sem("o_seeded"), sem("mix_done")
        mix_turned, mixT_act, mixT_dve, out_done = sem("mix_turned"), sem("mixT_act"), sem("mixT_dve"), sem("out_done")
        xb_landed, h_done, h_stored, h_squared, h_meaned, h_seeded = (sem("xb_landed"), sem("h_done"), sem("h_stored"),
                                                                      sem("h_squared"), sem("h_meaned"), sem("h_seeded"))
        hn_done, hn_turned, hnT_act, hnT_dve = sem("hn_done"), sem("hn_turned"), sem("hnT_act"), sem("hnT_dve")
        pq_done, pq_copied, sub_in_b = sem("pq_done"), sem("pq_copied"), sem("sub_in_b")
        sc_done, sc_copied = sem("sc_done"), sem("sc_copied")
        best_shifted, best_exp, topk_done = sem("best_shifted"), sem("best_exp"), sem("topk_done")

        idx_moved, idx_staged, idx_step = sem("idx_moved"), sem("idx_staged"), sem("idx_step")
        u_landed = [sem(f"u_landed{k}") for k in range(GS)]
        v_landed = [sem(f"v_landed{k}") for k in range(GS)]
        dotted = sem("dotted")
        v_used = sem("v_used")
        diag_done = sem("diag_done")
        gelu_arg, gelu_exp, act_done = sem("gelu_arg"), sem("gelu_exp"), sem("act_done")
        h_back, y_done, y_stored = sem("h_back"), sem("y_done"), sem("y_stored")

        n1w = vecs[:, 0:8]
        R_OUT, R_CONV, R_GOUT, R_Q, R_K = 8, 12, 60, 61, 62
        vec_loads = [(vec_rows[0:8, :], norm1_w[0].rearrange("(k p) -> k p", p=P)),
                     (vec_rows[R_OUT:R_OUT + 4, :], sb_out_norm_w[0].rearrange("(k p) -> k p", p=P)),
                     (vec_rows[R_CONV:R_CONV + 48, :], gdn_conv_w[0].rearrange("k (c p) -> (k c) p", p=P)),
                     (vec_rows[R_GOUT:R_GOUT + 1, :], gdn_out_norm_w[0:1, :]),
                     (vec_rows[R_Q:R_Q + 1, 0:64], sb_q_norm_w[0:1, :]), (vec_rows[R_Q:R_Q + 1, 64:128], sb_q_norm_w[0:1, :]),
                     (vec_rows[R_K:R_K + 1, 0:64], sb_k_norm_w[0:1, :]), (vec_rows[R_K:R_K + 1, 64:128], sb_k_norm_w[0:1, :]),
                     (dt_b[:, :], gdn_dt_bias[0:1, :].to_broadcast([P, GH])),
                     (a_neg[:, :], gdn_a_log[0:1, :].to_broadcast([P, GH])),
                     (norm2b[:, :], norm2_w[0:1, :].to_broadcast([P, D]))]

        block = ctx.enter_context(nc.Block())

        def known(e):
            e.wait_ge(consts, 1)

        def settled(e, value):
            if not isinstance(value, int):
                value = e.snap(value)
                e.compute_val(value)
            return value

        def steps_before(b):
            return b * (b + 1) // 2

        def py_loop(e, b, body):
            for t in range(1, b + 1):
                body(t)

        def fori_loop(e, b, body):
            with e.Fori(1, b + 1) as t:
                body(t)

        @block.sync
        def _(sp):
            for n in range(2):
                sp.dma_start(x_all[:, 4 * n:4 * n + 4, :],
                             x_blk[4 * n:4 * n + 4].rearrange("n p d -> p n d")).then_inc(x_landed[n], 16)
            sp.wait_ge(vec_clear, 1)
            for dst, src in vec_loads:
                sp.dma_start(dst, src).then_inc(consts_loaded, 16)
            for n, keys in enumerate((peer_sub_keys_1, peer_sub_keys_2)):
                sp.dma_start(heads(sub_in[n], PH), keys[0].rearrange("h k d -> k h d")).then_inc(sub_landed[n], 16)
            for n in range(2):
                sp.wait_ge(sub_copied, n + 1)
                sp.dma_start(d_subT.rearrange("p (h c) k -> p h c k", c=2)[:, :, n, :],
                             heads(sub_out[n], PH)).then_inc(sub_stored, 16)
            with sp.Fori(0, 2) as half:
                for n in range(NCH + 2):
                    m = n - 2
                    if m >= 0 and needs_tokens(m):
                        t = token_count(m) - 1
                        dst = d_gv if CH[m][0] == "v" else d_gk
                        sp.wait_ge(turned_copied, 8 * half + t + 1)
                        sp.dma_start(dst[bass.ds(half * 4, 4), :, CH[m][1] % 4, :].rearrange("b t c -> t b c"),
                                     tok_ring[t % 2].rearrange("p (b c) -> p b c", b=4)).then_inc(tok_stored[t % 2], 16)
                    if n < NCH and CH[n][0] != "v":
                        kind, c, _ = CH[n]
                        dst = {("g", 0): d_gqT, ("g", 1): d_gkT, ("s", 0): d_qT, ("s", 1): d_kT}[kind, c // 4]
                        sp.wait_ge(normed, NCH * half + n + 1)
                        sp.dma_start(dst[bass.ds(half * 4, 4), :, c % 4, :].rearrange("b p t -> p b t"),
                                     o_ring[n % 4].rearrange("p (b t) -> p b t", b=4)).then_inc(o_stored[n % 4], 16)
            def store_pair(a0):
                for p in range(2):
                    sp.wait_ge(v_copied, a0 + p + 3)
                    sp.dma_start(d_v[a0 + p], v_out[p]).then_inc(a2_stored[p], 16)
                    sp.wait_ge(gate_done, a0 + p + 3)
                    sp.dma_start(d_gate[a0 + p], g_out[p]).then_inc(a2_stored[p], 16)
                    sp.wait_ge(ab_done, a0 + p + 3)
                    sp.dma_start(d_ab[a0 + p], ab_out[p]).then_inc(a2_stored[p], 16)

            with sp.Fori(0, NB // 2 - 1) as pr:
                store_pair(pr * 2)
            for n in range(4):
                sp.wait_ge(o_stored[n], 32 * stores_before(NCH, n))
            for n in range(2):
                sp.wait_ge(tok_stored[n], 16 * 8)
                sp.wait_ge(a2_stored[n], 24 * (NB - 2))
            sp.wait_ge(x_staged, NB)

            def key_block(t, j):
                sp.wait_ge(z_done[0], t)
                sp.wait_ge(z_done[1], t)
                sp.dma_start(kTj, d_kT[j].rearrange("p h c -> p (h c)")).then_inc(k_landed, 16)
                sp.wait_ge(pv_done[0], t)
                sp.wait_ge(pv_done[1], t)
                sp.dma_start(vj, d_v[j]).then_inc(vj_landed, 16)

            def mix_loads(b):
                t0 = steps_before(b)
                count = settled(sp, b)
                known(sp)
                sp.wait_ge(mix_done, count)
                sp.wait_ge(sc_done, 4 * b)
                for dst, src in ((ab_in[:, :], d_ab), (gkT, d_gkT), (gqT, d_gqT), (gk, d_gk), (gv, d_gv)):
                    s2 = src[b] if len(src.shape) == 3 else src[b].rearrange("p h c -> p (h c)")
                    sp.dma_start(dst, s2).then_inc(gdn_landed, 16)
                sp.dma_start(gate, d_gate[b]).then_inc(gdn_landed, 16)
                sp.wait_ge(h_done, b)
                sp.dma_start(qT, d_qT[b].rearrange("p h c -> p (h c)")).then_inc(q_landed, 16)

                key_block(t0, b)

            def mix_tail(b):
                t1 = steps_before(b + 1)
                sp.wait_ge(z_done[0], t1)
                sp.wait_ge(z_done[1], t1)
                sp.dma_start(x_in, x_blk[b]).then_inc(xb_landed, 16)
                sp.wait_ge(mix_done, b + 1)
                sp.dma_start(T(0, 4), d_subT.rearrange("p h k -> p (h k)")).then_inc(sub_in_b, 16)
                sp.wait_ge(h_done, b + 1)
                sp.dma_start(d_h[b], h_sb).then_inc(h_stored, 16)

            def h_reload(n):
                sp.dma_start(y_buf, d_h[n]).then_inc(h_back, 16)

            def y_store(n):
                sp.wait_ge(y_done, n + 1)
                sp.dma_start(out_blk[n], y_buf).then_inc(y_stored, 16)

            def key_blocks(b, t0, loop):
                loop(sp, b, lambda t: key_block(t0 + t, b - t if isinstance(b, int) else nc.s_assert_within(
                    b - t, 0, NB - 1, skip_runtime_bounds_check_because="t runs from 1 to b")))

            def iteration(i, loop):
                key_blocks(i, steps_before(i), loop)
                mix_tail(i)
                if not isinstance(i, int) or i < NB - 1:
                    mix_loads(i + 1)

            mix_loads(0)
            store_pair(NB - 2)
            sp.wait_ge(tok_projected, NB)
            sp.dma_start(w_out_sb, w_out[0].rearrange("(k p) n -> p k n", p=P)).then_inc(wout_landed, 16)
            sp.dma_start(w_q_sb, peer_w_q[0].rearrange("(k p) n -> p k n", p=P)).then_inc(wq_landed, 16)
            for n in range(2):
                sp.wait_ge(a2_stored[n], 24 * NB)
            iteration(0, py_loop)
            iteration(1, py_loop)
            sp.wait_ge(h_stored, 16)
            h_reload(0)
            with sp.Fori(2, NB - 1) as i:
                iteration(i, fori_loop)
                y_store(i - 2)
                of_h, of_y = settled(sp, 16 * i), settled(sp, 16 * (i - 1))
                known(sp)
                sp.wait_ge(h_stored, of_h)
                sp.wait_ge(y_stored, of_y)
                h_reload(i - 1)
            for i in range(NB - 1, NB + 2):
                if i == NB - 1:
                    iteration(i, py_loop)
                y_store(i - 2)
                if i <= NB:
                    sp.wait_ge(y_stored, 16 * (i - 1))
                    sp.wait_ge(h_stored, 16 * i)
                    h_reload(i - 1)
            sp.wait_ge(y_stored, 16 * NB)

        @block.gpsimd
        def _(pool):
            g = nc.gpsimd
            g.memset(ident[:, :], 0.0)
            g.memset(ones[:, :], 1.0)
            g.memset(later[:, :], 1.0)
            g.memset(rest[:, :], 1.0)
            g.memset(visible[:, :], 1.0)
            g.memset(hidden[:, :], NEG)
            g.memset(upto[:, :], 1.0)
            g.memset(levels[:, :, :], 0.0)
            g.memset(mean64[:, :], 1.0 / SBD).then_inc(mask_step, 1)
            pool.wait_ge(mask_step, 1)
            for lv in range(6):
                s = 1 << lv
                g.memset(levels[:, lv, :].rearrange("p (a c) -> p a c", c=2 * s)[:, :, s:2 * s], 1.0)
            g.iota(iota16[:, :], [[1, TOPK]], base=0, channel_multiplier=0,
                   allow_small_or_imprecise_dtypes=True).then_inc(mask_step, 1)
            pool.wait_ge(mask_step, 2)

            def select(m, op, base, pattern, cm, fill=0.0):
                return g.affine_select(out=m, in_=m, compare_op=op, fill=fill, base=base, pattern=pattern,
                                       channel_multiplier=cm)

            select(ident[:, :], ALU.not_equal, 0, [[-1, P]], 1, 1.0)
            select(later[:, :], ALU.is_gt, 0, [[-1, P]], 1)
            select(rest[:, :], ALU.is_ge, 0, [[1, P]], -1)
            select(visible[:, :], ALU.is_gt, 0, [[1, P]], -1)
            select(hidden[:, :], ALU.is_ge, 0, [[-1, P]], 1)
            select(upto[:, :], ALU.is_ge, 0, [[1, P]], -1)
            select(mean64[:, 0:64], ALU.is_ge, 63, [[0, 64]], -1)
            select(mean64[:, 64:128], ALU.is_ge, -64, [[0, 64]], 1)
            for lv in range(6):
                s = 1 << lv
                m = levels[:, lv, :].rearrange("p (a c) -> p a c", c=2 * s)[:, :, s:2 * s]
                last = select(m, ALU.is_ge, 0, [[-2 * s, P // (2 * s)], [0, s]], 1)
            last.then_inc(mask_step, 1)
            pool.wait_ge(mask_step, 3)
            select(upto[:, 64:128], ALU.is_ge, -64, [[0, 64]], 1)
            for lv in range(6):
                s = 1 << lv
                m = levels[:, lv, :].rearrange("p (a c) -> p a c", c=2 * s)[:, :, s:2 * s]
                last = select(m, ALU.is_ge, s - 1, [[2 * s, P // (2 * s)], [0, s]], -1)
            last.then_inc(consts, 1)

            def gathers(i, do_u, do_v):
                if do_v:
                    count = settled(pool, i - 1)
                    known(pool)
                    pool.wait_ge(idx_moved, count)
                    mv = nc.gpsimd.tensor_copy(idx_v[:, :], idx_u[:, :])
                    if not do_u:
                        mv.then_inc(idx_moved, 1)
                if do_u:
                    if do_v:
                        mv.then_inc(idx_step, 1)
                        count = settled(pool, i - 1)
                        known(pool)
                        pool.wait_ge(idx_step, count)
                    else:
                        known(pool)
                    pool.wait_ge(topk_done, i)
                    nc.gpsimd.tensor_copy(idx_u[:, :], idx_new[:, :]).then_inc(idx_moved, 1)
                known(pool)
                pool.wait_ge(idx_moved, i)
                with pool.Fori(0, NG // 2) as pr:
                    g0 = pr * 2
                    for p in range(2):
                        gg = g0 + p
                        if do_u:
                            c = nc.gpsimd.tensor_copy(stage_u[p][:, :], idx_u[:, bass.ds(gg * GS, GS)])
                        if do_v:
                            c = nc.gpsimd.tensor_copy(stage_v[p][:, :], idx_v[:, bass.ds(gg * GS, GS)])
                        c.then_inc(idx_staged, 1)
                        pool.wait_ge(idx_staged, NG * (i - 1) + gg + 1)
                        for k in range(GS):
                            if do_u:
                                count = settled(pool, GS * (NG * (i - 1) + gg) + k + 1)
                                known(pool)
                                pool.wait_ge(dotted, count)
                                nc.gpsimd.indirect_dma_start(
                                    u_ring[:, k, :], None, u_rows,
                                    bass.IndirectOffsetOnAxis(stage_u[p][:, k:k + 1], 0)).then_inc(u_landed[k], 16)
                            if do_v:
                                count = settled(pool, GS * (NG * (i - 2) + gg) + k + 1)
                                known(pool)
                                pool.wait_ge(v_used, count)
                                nc.gpsimd.indirect_dma_start(
                                    v_ring[:, k, :], None, v_rows,
                                    bass.IndirectOffsetOnAxis(stage_v[p][:, k:k + 1], 0)).then_inc(v_landed[k], 16)

            gathers(1, True, False)
            with pool.Fori(2, NB) as i:
                gathers(i, True, True)
            gathers(NB, True, True)
            gathers(NB + 1, False, True)

        @block.scalar
        def _(act):
            a = nc.scalar
            act.wait_ge(x_landed[0], 16)
            for k in range(KC):
                act.dma_start(w_in_sb[:, k, :], w_in[0, k * P:(k + 1) * P, :]).then_inc(w_in_landed[k], 16)
            a.nop().then_inc(v_copied, 2)
            act.preload_act_table_set("natural_log_exp_and_others")
            for n in range(NB):
                if n % 4 == 0:
                    act.wait_ge(x_landed[n // 4], 16)
                if n:
                    act.drain()
                a.activation(work[:, 0:D], x_all[:, n, :], ACT.Square, accum_out=ss8[:, n:n + 1])
            act.drain()
            a.activation(y8[:, 0:1], ss8[:, 0:1], ACT.Copy).then_inc(x_squared, 1)
            act.wait_ge(x_meaned, 1)
            a.activation(y8, ms8, ACT.Ln)
            act.drain()
            a.activation(y8, y8, ACT.Exp, scale=-0.5).then_inc(x_seeded, 1)
            act.wait_ge(consts_loaded, 16 * len(vec_loads))
            a.activation(a_neg[:, :], a_neg[:, :], ACT.Exp).then_inc(vec_consts, 1)
            for n in range(NB):
                act.wait_ge(x_turned, n + 1)
                a.activation(xT[:, 0:4, n * P:(n + 1) * P], heads(bank(zz if n % 2 == 0 else rr, 0), 4),
                             ACT.Copy).then_inc(xT_act, 1)
            for n in range(2):
                act.wait_ge(sub_turned, n + 1)
                a.activation(sub_out[n], (ox, zz)[n][:, :], ACT.Copy).then_inc(sub_copied, 1)
            act.wait_ge(vecs_ready, 1)
            for k in ACT_CHUNKS:
                act.wait_ge(w_in_landed[k], 16)
                a.activation(w_in_sb[:, k, :], w_in_sb[:, k, :], ACT.Copy, scale=n1w[:, k:k + 1]).then_inc(w_in_scaled_act, 1)
            with act.Fori(0, 2) as half:
                for n in range(NCH + 8):
                    if n < NCH:
                        act.wait_ge(projected, NCH * half + n + 1)
                        if CH[n][0] == "s":
                            if n >= 6:
                                act.wait_ge(normed, NCH * half + n - 5)
                            a.activation(s_ring[n % 6], mm_bank[n % 2], ACT.Copy).then_inc(evacuated, 1)
                        else:
                            c = conv_count(n) - 1
                            if c >= 2:
                                act.wait_ge(convolved, 12 * half + c - 1)
                            a.activation(cb[c % 2][:, 3:515], mm_bank[n % 2], ACT.Copy).then_inc(evacuated, 1)
                    m = n - 1
                    if 0 <= m < NCH and CH[m][0] != "s":
                        c = conv_count(m) - 1
                        act.wait_ge(convolved, 12 * half + c + 1)
                        a.activation(e_ring[c % 2], s_ring[m % 6], ACT.Exp, scale=-1.0).then_inc(exp_done, 1)
                    m = n - 2
                    if 0 <= m < NCH and CH[m][0] != "v":
                        c = norm_count(m) - 1
                        if CH[m][0] == "g":
                            act.wait_ge(silu_done, 12 * half + conv_count(m))
                        else:
                            act.drain()
                        if c >= 2:
                            act.wait_ge(summed, 16 * half + c - 1)
                        a.activation(sq_ring[c % 2], s_ring[m % 6], ACT.Square).then_inc(squared, 1)
                    m = n - 4
                    if 0 <= m < NCH and CH[m][0] != "v":
                        c = norm_count(m) - 1
                        act.wait_ge(summed, 16 * half + c + 1)
                        if c >= 2:
                            act.wait_ge(normed, NCH * half + m - 1)
                        a.activation(y_ring[c % 2], ss_bank[c % 3], ACT.Ln, bias=EPS)
                        act.drain()
                        a.activation(y_ring[c % 2], y_ring[c % 2], ACT.Exp, scale=-0.5).then_inc(seeded, 1)
                    m = n - 7
                    if 0 <= m < NCH and needs_tokens(m):
                        t = token_count(m) - 1
                        act.wait_ge(turned, 8 * half + t + 1)
                        if t >= 2:
                            act.wait_ge(tok_stored[t % 2], 16 * (4 * half + t // 2))
                        a.activation(tok_ring[t % 2], tr_bank[t % 2], ACT.Copy).then_inc(turned_copied, 1)
                all_normed, all_stored = settled(act, NCH * half + NCH), settled(act, 64 * half + 64)
                known(act)
                act.wait_ge(normed, all_normed)
                for n in range(2):
                    act.wait_ge(tok_stored[n], all_stored)
            for n in range(4):
                act.wait_ge(o_stored[n], 32 * stores_before(NCH, n))
            for p in range(2):
                a.activation(stage_x[p], xT[:, :, p * P:(p + 1) * P], ACT.Copy).then_inc(x_staged, 1)

            def pair(a0, more):
                for p in range(2):
                    count = settled(act, a0 + p + 1)
                    known(act)
                    act.wait_ge(tok_projected, count)
                    if more:
                        a.activation(stage_x[p], xT[:, :, bass.ds((a0 + 2 + p) * P, P)], ACT.Copy).then_inc(x_staged, 1)
                    a.activation(v_out[p], av_bank[p], ACT.Copy).then_inc(v_copied, 1)
                    a.activation(g_exp[p], ag_bank[p], ACT.Exp, scale=-1.0)
                    a.activation(ab_e[p][:, 4:8], ab_bank[p][:, 4:8], ACT.Exp, scale=-1.0).then_inc(gate_exp, 1)
                    act.wait_ge(ab_sum, a0 + p + 1)
                    a.activation(ab_e[p][:, 0:4], ab_e[p][:, 0:4], ACT.Exp)
                    act.drain()
                    a.activation(ab_e[p][:, 0:4], ab_e[p][:, 0:4], ACT.Ln, bias=1.0).then_inc(ab_exp, 1)
                after = settled(act, 24 * a0 + 48)
                known(act)
                for p in range(2):
                    act.wait_ge(a2_stored[p], after)

            with act.Fori(0, NB // 2 - 1) as pr:
                pair(pr * 2, True)
            pair(NB - 2, False)

            def fill(i, g, v):
                if not v:
                    return
                for k in range(GS):
                    n = GS * (NG * (i - 2) + g) + k + 1
                    act.wait_ge(v_used, n)
                    known(act)
                    a.activation(diag[:, k, :], ident[:, :], ACT.Copy,
                                 scale=act_w[:, bass.ds(g * GS + k, 1)]).then_inc(diag_done, 1)

            def seed(y, ms, s):
                a.activation(y, ms, ACT.Ln)
                act.drain()
                a.activation(y, y, ACT.Exp, scale=-0.5).then_inc(s, 1)

            def mixing(b, i, v, loop):
                t0 = steps_before(b)
                fill(i, 0, v)
                act.wait_ge(ex_ready, b + 1)
                a.activation(ex, ex_in, ACT.Exp).then_inc(ex_done, 1)
                act.wait_ge(spread_done, b + 1)
                a.activation(t_qd, bank(zz, 0), ACT.Exp).then_inc(qd_exp, 1)
                act.wait_ge(decay_arg, b + 1)
                a.activation(t_dt, t_dt, ACT.Exp).then_inc(decay_exp, 1)
                act.wait_ge(tt_turned, b + 1)
                a.activation(t_T, bank(ox, 1), ACT.Copy).then_inc(tt_copied, 1)
                fill(i, 1, v)
                for lv in range(1, 6):
                    act.wait_ge(p_done, 5 * b + lv)
                    a.activation(t_p, bank(zz, 0), ACT.Copy).then_inc(p_copied, 1)
                    fill(i, 1 + lv, v)
                act.wait_ge(uw_done, b + 1)
                a.activation(t_u, bank(rr, 1), ACT.Copy)
                a.activation(t_wT, bank(ox, 1), ACT.Copy).then_inc(uw_copied, 1)
                fill(i, 7, v)
                fill(i, 8, v)
                act.wait_ge(og_done, b + 1)
                a.activation(mix[:, 512:1024], bank(ox, 0), ACT.Copy).then_inc(og_copied, 1)

                def key_step(t, g):
                    fill(i, g, v)
                    for hg in range(2):
                        act.wait_ge(z_done[hg], t + 1)
                        a.activation(att_l[hg], bank(zz, hg), ACT.Abs)
                        act.drain()
                        a.activation(att_l[hg], att_l[hg], ACT.Exp, scale=-1.0)
                        act.drain()
                        a.activation(att_l[hg], att_l[hg], ACT.Ln, bias=1.0).then_inc(l_done[hg], 1)
                    for hg in range(2):
                        act.wait_ge(arg_done[hg], t + 1)
                        a.activation(att_u[hg], att_u[hg], ACT.Exp).then_inc(w_done[hg], 1)

                key_step(t0, 9)
                loop(act, b, lambda t: key_step(t0 + t, 9 + t))
                for hg in range(2):
                    act.wait_ge(pv_done[hg], t0 + b + 1)
                a.activation(sq_att, bank(ox, 0), ACT.Square)
                a.activation(sq_gdn, mix[:, 512:1024], ACT.Square).then_inc(o_squared, 1)
                g = 10 + b
                fill(i, g, v)
                act.wait_ge(o_meaned, b + 1)
                seed(y12, ms12, o_seeded)
                act.wait_ge(mix_turned, b + 1)
                a.activation(mixT[:, 0:512], bank(rr, 0), ACT.Copy).then_inc(mixT_act, 1)
                fill(i, g + 1, v)
                act.wait_ge(h_done, b + 1)
                a.activation(sq_h, h_sb, ACT.Square, accum_out=ssh)
                act.drain()
                a.activation(yh, ssh, ACT.Copy).then_inc(h_squared, 1)
                act.wait_ge(h_meaned, b + 1)
                seed(yh, msh, h_seeded)
                fill(i, g + 2, v)
                act.wait_ge(hn_turned, b + 1)
                a.activation(hnT[:, 0:512], bank(rr, 0), ACT.Copy).then_inc(hnT_act, 1)
                for q in range(4):
                    act.wait_ge(pq_done, 4 * b + q + 1)
                    a.activation(pqT[:, 4 * q:4 * q + 4, :], heads(bank(zz if q < 2 else rr, q % 2), 4),
                                 ACT.Copy).then_inc(pq_copied, 1)
                    fill(i, g + 3 + q, v)
                act.wait_ge(h_stored, 16 * (b + 1))
                for q in range(4):
                    act.wait_ge(sc_done, 4 * b + q + 1)
                    a.activation(sc[:, 2 * q:2 * q + 2, :, :],
                                 bank(zz if q < 2 else rr, q % 2).rearrange("p (h c k) -> p h c k", h=2, c=2),
                                 ACT.Copy).then_inc(sc_copied, 1)
                for q in range(7):
                    fill(i, g + 7 + q, v)
                act.wait_ge(best_shifted, b + 1)
                a.activation(best, best, ACT.Exp).then_inc(best_exp, 1)
                return g + 14

            def ending(i, u):
                if u:
                    act.wait_ge(gelu_arg, i)
                    a.activation(gelu_t[:, :], gelu_t[:, :], ACT.Exp, scale=-2.0 * GELU_S).then_inc(gelu_exp, 1)

            def rest_groups(i, g, v):
                with act.Fori(g, NG) as gg:
                    fill(i, gg, v)

            mixing(0, 0, False, py_loop)
            mixing(1, 1, False, py_loop)
            ending(1, True)
            with act.Fori(2, NB) as i:
                act.wait_ge(act_done, i - 1)
                g = mixing(i, i, True, fori_loop)
                rest_groups(i, g, True)
                ending(i, True)
            act.wait_ge(act_done, NB - 1)
            rest_groups(NB, 0, True)
            ending(NB, True)
            act.wait_ge(act_done, NB)
            rest_groups(NB + 1, 0, True)

        @block.vector
        def _(dve):
            v = nc.vector

            def spread(ap, h, n):
                return ap.unsqueeze(2).to_broadcast([P, h, n])

            def every(ap, h):
                return ap.unsqueeze(1).to_broadcast([P, h, ap.shape[1]])

            def newton(r, y, ms, a):
                v.tensor_tensor(a, y, y, ALU.mult)
                dve.drain()
                v.tensor_tensor(a, a, ms, ALU.mult)
                dve.drain()
                v.scalar_tensor_tensor(r, a, -3.0, y, ALU.add, ALU.mult)
                dve.drain()

            def one_over_one_plus(e):
                v.tensor_scalar(e, e, 1.0, BIG, ALU.add, ALU.min)
                dve.drain()
                v.reciprocal(e, e)
                dve.drain()

            v.memset(vec_rows, 0.0).then_inc(vec_clear, 1)
            v.nop().then_inc(gate_done, 2)
            v.nop().then_inc(ab_done, 2)
            dve.wait_ge(x_squared, 1)
            v.tensor_scalar(ms8, ss8, 1.0 / D, EPS, ALU.mult, ALU.add).then_inc(x_meaned, 1)
            dve.wait_ge(x_seeded, 1)
            newton(r8, y8, ms8, a8)
            for n in range(NB):
                v.tensor_scalar(x_all[:, n, :], x_all[:, n, :], r8[:, n:n + 1], -0.5, ALU.mult, ALU.mult).then_inc(x_scaled, 1)
            for n in range(NB):
                dve.wait_ge(x_turned, n + 1)
                v.tensor_copy(xT[:, 4:8, n * P:(n + 1) * P], heads(bank(zz if n % 2 == 0 else rr, 1), 4)).then_inc(xT_dve, 1)
            dve.wait_ge(vec_turned, 1)
            v.tensor_copy(vecs[:, :], bank(va, 1)[:, 0:P])
            dve.drain()
            v.tensor_scalar(vecs[:, R_Q:R_Q + 1], vecs[:, R_Q:R_Q + 1], -0.5 * SBD ** -0.5, None, ALU.mult)
            v.tensor_scalar(vecs[:, R_K:R_K + 1], vecs[:, R_K:R_K + 1], -0.5, None, ALU.mult).then_inc(vecs_ready, 1)
            for k in [k for k in range(KC) if k not in ACT_CHUNKS]:
                dve.wait_ge(w_in_landed[k], 16)
                v.tensor_scalar(w_in_sb[:, k, :], w_in_sb[:, k, :], n1w[:, k:k + 1], None, ALU.mult).then_inc(w_in_scaled, 1)
            dve.wait_ge(sub_stored, 32)
            v.memset(hist, 0.0).then_inc(dotted, GS)
            dve.drain()
            with dve.Fori(0, 2) as half:
                for n in range(NCH + 8):
                    if n < NCH and CH[n][0] != "s":
                        c = conv_count(n) - 1
                        w = [R_CONV + 12 * k + CH[n][1] + (8 if CH[n][0] == "v" else 0) for k in range(TAPS)]
                        dve.wait_ge(evacuated, NCH * half + n + 1)
                        v.tensor_copy(cb[c % 2][:, 0:3], hist[:, c, :])
                        dve.drain()
                        v.tensor_copy(hist[:, c, :], cb[c % 2][:, 512:515])
                        v.tensor_scalar(s_ring[n % 6], cb[c % 2][:, 3:515], vecs[:, w[3]:w[3] + 1], None, ALU.mult)
                        for k in (2, 1, 0):
                            dve.drain()
                            last = v.scalar_tensor_tensor(s_ring[n % 6], cb[c % 2][:, k:k + 512], vecs[:, w[k]:w[k] + 1],
                                                          s_ring[n % 6], ALU.mult, ALU.add)
                        last.then_inc(convolved, 1)
                    m = n - 1
                    if 0 <= m < NCH and CH[m][0] != "s":
                        c = conv_count(m) - 1
                        dve.wait_ge(exp_done, 12 * half + c + 1)
                        one_over_one_plus(e_ring[c % 2])
                        v.tensor_tensor(s_ring[m % 6], s_ring[m % 6], e_ring[c % 2], ALU.mult).then_inc(silu_done, 1)
                    m = n - 5
                    if 0 <= m < NCH:
                        kind, ck, _ = CH[m]
                        if kind != "v":
                            c = norm_count(m) - 1
                            y, t0, t1 = y_ring[c % 2], tmp_a[0], tmp_a[1]
                            dve.drain()
                            dve.wait_ge(seeded, 16 * half + c + 1)
                            v.tensor_tensor(t0, y, y, ALU.mult)
                            dve.drain()
                            v.scalar_tensor_tensor(t1, ss_bank[c % 3], EPS, t0, ALU.add, ALU.mult)
                            dve.drain()
                            v.scalar_tensor_tensor(t0, t1, -3.0, y, ALU.add, ALU.mult)
                            scale = (vecs[:, R_Q + ck // 4:R_Q + ck // 4 + 1] if kind == "s"
                                     else -0.5 * (GD ** -0.5 if ck < GH else 1.0))
                        dve.drain()
                        if stores_before(m, m % 4):
                            dve.wait_ge(o_stored[m % 4],
                                        16 * (stores_before(NCH, m % 4) * half + stores_before(m, m % 4)))
                        if m >= 4 and needs_tokens(m - 4):
                            dve.wait_ge(turned, 8 * half + token_count(m - 4))
                        if kind != "v":
                            v.scalar_tensor_tensor(o_ring[m % 4], s_ring[m % 6], scale, t0, ALU.mult, ALU.mult).then_inc(normed, 1)
                        else:
                            v.tensor_copy(o_ring[m % 4], s_ring[m % 6]).then_inc(normed, 1)
                all_stored = [settled(dve, 16 * stores_before(NCH, n) * (half + 1)) for n in range(4)]
                all_turned = settled(dve, 8 * half + 8)
                known(dve)
                for n in range(4):
                    dve.wait_ge(o_stored[n], all_stored[n])
                dve.wait_ge(turned, all_turned)
            dve.wait_ge(vec_consts, 1)
            dve.wait_ge(turned_copied, 16)
            with dve.Fori(0, NB // 2) as pr:
                a0 = pr * 2
                for p in range(2):
                    dve.wait_ge(gate_exp, a0 + p + 1)
                    v.tensor_tensor(ab_y[p], ab_bank[p][:, 0:4], dt_b[:, :], ALU.add)
                    dve.drain()
                    v.scalar_tensor_tensor(ab_e[p][:, 0:4], ab_y[p], -1.0, ab_y[p], ALU.mult, ALU.min).then_inc(ab_sum, 1)
                    one_over_one_plus(g_exp[p])
                    v.tensor_tensor(g_out[p], ag_bank[p], g_exp[p], ALU.mult).then_inc(gate_done, 1)
                    dve.wait_ge(ab_exp, a0 + p + 1)
                    v.scalar_tensor_tensor(ab_out[p][:, 0:4], ab_y[p], 0.0, ab_e[p][:, 0:4], ALU.max, ALU.add)
                    one_over_one_plus(ab_e[p][:, 4:8])
                    v.tensor_copy(ab_out[p][:, 4:8], ab_e[p][:, 4:8])
                    v.scalar_tensor_tensor(ab_out[p][:, 0:4], ab_out[p][:, 0:4], -1.0, a_neg[:, :], ALU.mult, ALU.mult).then_inc(ab_done, 1)
                after = settled(dve, 24 * a0 + 48)
                known(dve)
                for p in range(2):
                    dve.wait_ge(a2_stored[p], after)

            v.memset(g_sel, 0.0)
            dve.drain()

            def fill(i, g, u, slots=range(GS)):
                if not u:
                    return
                for k in slots:
                    dve.wait_ge(u_landed[k], 16 * (NG * (i - 1) + g + 1))
                    v.scalar_tensor_tensor(u_ring[:, k, :], u_ring[:, k, :], 1.0, hn_cur, ALU.mult, ALU.mult,
                                           accum_out=dots[:, bass.ds(g * GS + k, 1)]).then_inc(dotted, 1)

            def mixing(b, i, u, loop):
                t0 = steps_before(b)
                beta = ab_in[:, GH:2 * GH]
                dve.wait_ge(gdn_landed, 96 * (b + 1))
                v.tensor_copy(g_sel[0:64, 0:4], ab_in[0:64, 0:4])
                v.tensor_copy(g_sel[64:128, 4:8], ab_in[64:128, 0:4]).then_inc(g_split, 1)
                if isinstance(b, int) and b == 0:
                    v.memset(state, 0.0)
                fill(i, 0, u, range(2))
                dve.wait_ge(g_summed, b + 1)
                v.tensor_copy(ex_in[:, 0:4], bank(ox, 1)[:, 0:4])
                v.tensor_copy(ex_in[:, 8:16], bank(ox, 1)[:, 4:12])
                dve.drain()
                v.tensor_tensor(ex_in[0:64, 4:8], ex_in[0:64, 8:12], ex_in[0:64, 0:4], ALU.subtract)
                v.tensor_tensor(ex_in[64:128, 4:8], ex_in[64:128, 12:16], ex_in[64:128, 0:4], ALU.subtract).then_inc(ex_ready, 1)
                v.tensor_tensor(heads(t_xt, 4), every(ident[:, :], 4), spread(ex_in[:, 0:4], 4, P), ALU.mult)
                v.tensor_tensor(heads(t_p, 4), every(ident[:, :], 4), spread(beta, 4, P), ALU.mult).then_inc(diags_ready, 1)
                fill(i, 0, u, range(2, GS))
                dve.wait_ge(qd_exp, b + 1)
                v.tensor_tensor(heads(t_dt, 4), heads(bank(zz, 0), 4), spread(ex_in[:, 0:4], 4, P), ALU.subtract)
                dve.drain()
                v.tensor_scalar(t_dt, t_dt, 0.0, None, ALU.min).then_inc(decay_arg, 1)
                dve.wait_ge(ex_done, b + 1)
                v.tensor_tensor(kbg_w, beta, ex[:, 0:4], ALU.mult)
                v.tensor_tensor(heads(t_vb, 4), heads(gv, 4), spread(beta, 4, P), ALU.mult)
                v.tensor_tensor(heads(t_kd, 4), heads(gk, 4), spread(ex[:, 4:8], 4, P), ALU.mult)
                dve.drain()
                v.tensor_tensor(heads(t_kbg, 4), heads(gk, 4), spread(kbg_w, 4, P), ALU.mult)
                dve.wait_ge(decay_exp, b + 1)
                v.tensor_tensor(heads(t_dt, 4), heads(t_dt, 4), every(upto[:, :], 4), ALU.mult)
                v.tensor_tensor(t_qd, t_qd, gqT, ALU.mult)
                dve.drain()
                v.tensor_tensor(t_at, t_dt, bank(zz, 1), ALU.mult)
                dve.drain()
                dve.wait_ge(pairs_done, b + 1)
                v.tensor_tensor(t_at, t_at, bank(rr, 0), ALU.mult)
                v.tensor_tensor(t_dt, t_dt, bank(rr, 1), ALU.mult)
                dve.drain()
                v.tensor_tensor(heads(t_xt, 4), heads(t_at, 4), every(levels[:, 0, :], 4), ALU.mult)
                dve.drain()
                v.tensor_tensor(heads(t_TT, 4), every(ident[:, :], 4), heads(t_xt, 4), ALU.subtract).then_inc(tt_first, 1)

                def next_level(lv):
                    dve.drain()
                    v.tensor_tensor(heads(t_xt, 4), heads(t_at, 4), every(levels[:, lv, :], 4), ALU.mult).then_inc(x_ready, 1)

                next_level(1)
                fill(i, 1, u)
                for lv in range(1, 6):
                    dve.wait_ge(corr_done, 5 * b + lv)
                    if lv < 5:
                        v.tensor_tensor(t_T, t_T, bank(zz, 1), ALU.subtract)
                    v.tensor_tensor(t_TT, t_TT, bank(rr, 0), ALU.subtract).then_inc(t_ready, 1)
                    if lv < 5:
                        next_level(lv + 1)
                    fill(i, 1 + lv, u)
                dve.wait_ge(uw_copied, b + 1)
                for c in range(2):
                    r = slice(64 * c, 64 * c + 64)
                    dve.wait_ge(ws_done, 2 * b + c + 1)
                    v.tensor_tensor(t_vn[r, :], t_u[r, :], bank(zz, 0)[r, :], ALU.subtract).then_inc(vn_ready, 1)
                    dve.drain()
                    dve.wait_ge(kv_done, 2 * b + c + 1)
                    for h in range(GH):
                        last = v.scalar_tensor_tensor(heads(state, 4)[:, h, :], heads(state, 4)[:, h, :],
                                                      ex[:, 8 + 4 * c + h:9 + 4 * c + h], heads(bank(zz, 1), 4)[:, h, :],
                                                      ALU.mult, ALU.add)
                    last.then_inc(state_ready, 1)
                    fill(i, 7 + c, u)

                def key_step(t, g, first=False):
                    fill(i, g, u)
                    for hg in range(2):
                        dve.wait_ge(l_done[hg], t + 1)
                        dve.wait_ge(rest_done[hg], t)
                        sp = v.scalar_tensor_tensor(att_sp[hg], bank(zz, hg), 0.0, att_l[hg], ALU.max, ALU.add)
                        if first:
                            dve.drain()
                            sp = v.tensor_tensor(heads(att_sp[hg], 4), heads(att_sp[hg], 4), every(visible[:, :], 4), ALU.mult)
                        sp.then_inc(sp_done[hg], 1)
                        dve.wait_ge(pv_done[hg], t)
                        v.scalar_tensor_tensor(att_u[hg], bank(zz, hg), 0.0, att_l[hg], ALU.min,
                                               ALU.subtract).then_inc(z_used[hg], 1)
                    for hg in range(2):
                        dve.drain()
                        dve.wait_ge(later_done[hg], t + 1)
                        arg = v.tensor_tensor(att_u[hg], att_u[hg], bank(rr, hg), ALU.subtract)
                        if first:
                            dve.drain()
                            arg = v.tensor_tensor(heads(att_u[hg], 4), heads(att_u[hg], 4), every(hidden[:, :], 4), ALU.add)
                        arg.then_inc(arg_done[hg], 1)

                key_step(t0, 9, first=True)
                loop(dve, b, lambda t: key_step(t0 + t, 9 + t))
                if isinstance(b, int) and b == 0:
                    dve.wait_ge(wout_landed, 16)
                    for k in range(KC):
                        col = R_OUT + k if k < 4 else R_GOUT
                        last = v.tensor_scalar(w_out_sb[:, k, :], w_out_sb[:, k, :], vecs[:, col:col + 1], None, ALU.mult)
                    last.then_inc(wout_scaled, 1)
                g = 10 + b
                fill(i, g, u, range(2))
                dve.wait_ge(o_squared, b + 1)
                v.tensor_reduce(ss12[:, 0:8], heads(sq_att, SBH), AX.X, ALU.add)
                v.tensor_reduce(ss12[:, 8:12], heads(sq_gdn, GH), AX.X, ALU.add)
                dve.drain()
                v.tensor_scalar(ms12[:, 0:8], ss12[:, 0:8], 1.0 / SBD, EPS, ALU.mult, ALU.add)
                v.tensor_scalar(ms12[:, 8:12], ss12[:, 8:12], 1.0 / GD, EPS, ALU.mult, ALU.add).then_inc(o_meaned, 1)
                dve.wait_ge(o_seeded, b + 1)
                newton(r12, y12, ms12, a12)
                v.tensor_scalar(r12, r12, -0.5, None, ALU.mult)
                dve.drain()
                v.tensor_tensor(heads(mix[:, 512:1024], GH), heads(mix[:, 512:1024], GH), spread(r12[:, 8:12], GH, GD), ALU.mult)
                v.tensor_tensor(heads(mix[:, 0:512], SBH), heads(bank(ox, 0), SBH), spread(r12[:, 0:8], SBH, SBD), ALU.mult)
                dve.drain()
                v.tensor_tensor(mix[:, 512:1024], mix[:, 512:1024], gate, ALU.mult).then_inc(mix_done, 1)
                fill(i, g, u, range(2, GS))
                dve.wait_ge(mix_turned, b + 1)
                v.tensor_copy(mixT[:, 512:1024], bank(rr, 1)).then_inc(mixT_dve, 1)
                fill(i, g + 1, u)
                dve.wait_ge(xb_landed, 16 * (b + 1))
                dve.wait_ge(out_done, b + 1)
                v.tensor_tensor(h_sb, zz[:, :], x_in, ALU.add).then_inc(h_done, 1)
                dve.wait_ge(h_squared, b + 1)
                v.tensor_scalar(msh, ssh, 1.0 / D, EPS, ALU.mult, ALU.add).then_inc(h_meaned, 1)
                dve.wait_ge(h_seeded, b + 1)
                newton(rh, yh, msh, ah)
                v.tensor_scalar(rh, rh, -0.5, None, ALU.mult)
                dve.drain()
                v.scalar_tensor_tensor(hn_new, h_sb, rh, norm2b[:, :], ALU.mult, ALU.mult).then_inc(hn_done, 1)
                fill(i, g + 2, u)
                dve.wait_ge(hn_turned, b + 1)
                v.tensor_copy(hnT[:, 512:1024], bank(rr, 1)).then_inc(hnT_dve, 1)
                for q in range(4):
                    fill(i, g + 3 + q, u)
                for q in range(4):
                    four = [(h, c) for h in (2 * q, 2 * q + 1) for c in range(2)]
                    count = settled(dve, 4 * b + q + 1)
                    known(dve)
                    dve.wait_ge(sc_copied, count)
                    for h, c in four:
                        v.max(top_v[:, h, c, 0:8], sc[:, h, c, :])
                    dve.drain()
                    for h, c in four:
                        v.max_index(top_i[:, h, c, 0:8], top_v[:, h, c, 0:8], sc[:, h, c, :])
                    dve.drain()
                    for h, c in four:
                        v.match_replace(sc[:, h, c, :], top_v[:, h, c, 0:8], sc[:, h, c, :], -BIG)
                    dve.drain()
                    for h, c in four:
                        v.max(top_v[:, h, c, 8:16], sc[:, h, c, :])
                    dve.drain()
                    for h, c in four:
                        v.max_index(top_i[:, h, c, 8:16], top_v[:, h, c, 8:16], sc[:, h, c, :])
                    fill(i, g + 7 + q, u)
                dve.drain()
                v.tensor_tensor(cand, top_v[:, :, 0, :].unsqueeze(3).to_broadcast([P, PH, TOPK, TOPK]),
                                top_v[:, :, 1, :].unsqueeze(2).to_broadcast([P, PH, TOPK, TOPK]), ALU.add)
                v.tensor_copy(top_f, top_i)
                dve.drain()
                flat = T(W + 4, 4).rearrange("p (h n) -> p h n", h=PH)
                for q in range(2):
                    hs = range(4 * q, 4 * q + 4)
                    for h in hs:
                        v.max(best[:, h, 0:8], flat[:, h, :])
                    dve.drain()
                    for h in hs:
                        v.max_index(ci[:, h, 0:8], best[:, h, 0:8], flat[:, h, :])
                    dve.drain()
                    for h in hs:
                        v.match_replace(flat[:, h, :], best[:, h, 0:8], flat[:, h, :], -BIG)
                    dve.drain()
                    for h in hs:
                        v.max(best[:, h, 8:16], flat[:, h, :])
                    dve.drain()
                    for h in hs:
                        v.max_index(ci[:, h, 8:16], best[:, h, 8:16], flat[:, h, :])
                    fill(i, g + 11 + q, u, range(GS) if q == 0 else range(2))
                dve.drain()
                v.tensor_copy(gsum, best[:, :, 0])
                ci_flat = small[:, 896:1024].bitcast(U32)
                v.tensor_scalar(ci_hi, ci_flat, 4, None, ALU.logical_shift_right)
                dve.drain()
                v.tensor_tensor(best, best, spread(gsum, PH, TOPK), ALU.subtract).then_inc(best_shifted, 1)
                for table, which, e in ((0, ci_hi, e1), (1, ci_flat, e2)):
                    if table:
                        dve.drain()
                        v.tensor_scalar(ci_flat, ci_flat, TOPK - 1, None, ALU.bitwise_and)
                        dve.drain()
                    v.tensor_copy(ci_f, which.rearrange("p (h k) -> p h k", h=PH))
                    dve.drain()
                    v.tensor_tensor(hot, ci_f.unsqueeze(3).to_broadcast([P, PH, TOPK, TOPK]),
                                    iota16[:, :].unsqueeze(1).unsqueeze(1).to_broadcast([P, PH, TOPK, TOPK]), ALU.is_equal)
                    dve.drain()
                    v.tensor_tensor(hot, hot, top_f[:, :, table, :].unsqueeze(2).to_broadcast([P, PH, TOPK, TOPK]), ALU.mult)
                    dve.drain()
                    v.tensor_reduce(e, hot, AX.X, ALU.add)
                    if table:
                        fill(i, g + 13, u)
                    else:
                        fill(i, g + 12, u, range(2, GS))
                dve.wait_ge(best_exp, b + 1)
                v.tensor_reduce(gsum, best, AX.X, ALU.add)
                dve.drain()
                v.reciprocal(gsum, gsum)
                dve.drain()
                v.tensor_tensor(gate_new[:, :].rearrange("p (h k) -> p h k", h=PH), best, spread(gsum, PH, TOPK), ALU.mult)
                dve.wait_ge(idx_moved, i)
                v.scalar_tensor_tensor(idx_new[:, :].rearrange("p (h k) -> p h k", h=PH), e1, float(NK), e2,
                                       ALU.mult, ALU.add).then_inc(topk_done, 1)
                return g + 14

            def ending(i, m, u, w):
                dve.drain()
                if u:
                    v.tensor_tensor(gelu_t[:, :], dots[:, :], dots[:, :], ALU.mult)
                    dve.drain()
                    v.tensor_scalar(gelu_t[:, :], gelu_t[:, :], GELU_C, 1.0, ALU.mult, ALU.add)
                    dve.drain()
                    v.tensor_tensor(gelu_t[:, :], gelu_t[:, :], dots[:, :], ALU.mult)
                    dve.drain()
                    v.tensor_scalar(gelu_t[:, :], gelu_t[:, :], -50.0, None, ALU.max).then_inc(gelu_arg, 1)
                    dve.wait_ge(gelu_exp, i)
                    one_over_one_plus(gelu_t[:, :])
                    v.tensor_tensor(gelu_t[:, :], gelu_t[:, :], dots[:, :], ALU.mult)
                    dve.drain()
                    if w:
                        dve.wait_ge(diag_done, SLOTS * (i - 1))
                    v.tensor_tensor(act_w[:, :], gelu_t[:, :], gate_cur[:, :], ALU.mult).then_inc(act_done, 1)
                    dve.drain()
                if m:
                    v.tensor_copy(gate_cur[:, :], gate_new[:, :])
                    v.tensor_copy(hn_cur, hn_new)
                    dve.drain()
                if w:
                    dve.wait_ge(h_back, 16 * (i - 1))
                    dve.wait_ge(v_used, GS + SLOTS * (i - 1))
                    v.tensor_tensor(y_buf, va[:, :], y_buf, ALU.add).then_inc(y_done, 1)

            def rest_groups(i, g, u):
                with dve.Fori(g, NG) as gg:
                    fill(i, gg, u)

            mixing(0, 0, False, py_loop)
            ending(0, True, False, False)
            g = mixing(1, 1, True, py_loop)
            rest_groups(1, g, True)
            ending(1, True, True, False)
            with dve.Fori(2, NB) as i:
                g = mixing(i, i, True, fori_loop)
                rest_groups(i, g, True)
                ending(i, True, True, True)
            rest_groups(NB, 0, True)
            ending(NB, False, True, True)
            ending(NB + 1, False, False, True)

        @block.tensor
        def _(pe):
            t_ = nc.tensor

            def mm(out_, lhsT, rhs, start=True, stop=True):
                return t_.matmul(out_, lhsT, rhs, start=start, stop=stop, skip_group_check=True)

            def turn(dst, src, n):
                for c in range(n):
                    last = t_.transpose(dst[:, c * P:(c + 1) * P], src[:, c * P:(c + 1) * P], ident[:, :])
                return last

            pe.wait_ge(consts, 1)
            t_.nop().then_inc(v_used, GS)
            for n in range(NB):
                pe.wait_ge(x_scaled, n + 1)
                if n >= 2:
                    pe.wait_ge(xT_act, n - 1)
                    pe.wait_ge(xT_dve, n - 1)
                turn((zz if n % 2 == 0 else rr)[:, :], x_all[:, n, :], KC).then_inc(x_turned, 1)
            pe.wait_ge(consts_loaded, 16 * len(vec_loads))
            turn(bank(va, 1), vec_rows, 1).then_inc(vec_turned, 1)
            for n in range(2):
                pe.wait_ge(sub_landed[n], 16)
                if n:
                    pe.wait_ge(xT_act, NB)
                    pe.wait_ge(xT_dve, NB)
                turn((ox, zz)[n][:, :], sub_in[n], PH).then_inc(sub_turned, 1)
            pe.wait_ge(w_in_scaled, KC - len(ACT_CHUNKS))
            pe.wait_ge(w_in_scaled_act, len(ACT_CHUNKS))
            pe.wait_ge(xT_act, NB)
            pe.wait_ge(xT_dve, NB)
            pe.wait_ge(sub_copied, 2)
            with pe.Fori(0, 2) as half:
                for n in range(NCH + 8):
                    if n < NCH:
                        col = CH[n][2]
                        if n >= 2:
                            pe.wait_ge(evacuated, NCH * half + n - 1)
                        for k in range(KC):
                            last = mm(mm_bank[n % 2], w_in_sb[:, k, col:col + P], xT[:, k, bass.ds(half * HALF, HALF)],
                                      k == 0, k == KC - 1)
                        last.then_inc(projected, 1)
                    m = n - 3
                    if 0 <= m < NCH and CH[m][0] != "v":
                        c = norm_count(m) - 1
                        if c >= 3:
                            pe.wait_ge(normed, NCH * half + m - 2)
                        pe.wait_ge(squared, 16 * half + c + 1)
                        mm(ss_bank[c % 3], (ones if CH[m][0] == "g" else mean64)[:, :], sq_ring[c % 2]).then_inc(summed, 1)
                    m = n - 6
                    if 0 <= m < NCH and needs_tokens(m):
                        t = token_count(m) - 1
                        pe.wait_ge(normed, NCH * half + m + 1)
                        if t >= 2:
                            pe.wait_ge(turned_copied, 8 * half + t - 1)
                        turn(tr_bank[t % 2], o_ring[m % 4], 4).then_inc(turned, 1)
                all_normed, all_turned = settled(pe, NCH * half + NCH), settled(pe, 8 * half + 8)
                known(pe)
                pe.wait_ge(normed, all_normed)
                pe.wait_ge(turned_copied, all_turned)
            with pe.Fori(0, NB // 2) as pr:
                a0 = pr * 2
                for p in range(2):
                    pe.wait_ge(v_copied, a0 + p + 1)
                    pe.wait_ge(gate_done, a0 + p + 1)
                    pe.wait_ge(ab_done, a0 + p + 1)
                    pe.wait_ge(x_staged, a0 + p + 1)
                    for bk, c0, n in ((av_bank[p], COL_SV, SBW), (ag_bank[p], COL_GATE, GW), (ab_bank[p], COL_AB, 2 * GH)):
                        for k in range(KC):
                            last = mm(bk, stage_x[p][:, k, :], w_in_sb[:, k, c0:c0 + n], k == 0, k == KC - 1)
                    last.then_inc(tok_projected, 1)
            def fill(i, g, v, first=False, slots=range(GS)):
                if not v:
                    return
                for k in slots:
                    pe.wait_ge(v_landed[k], 16 * (NG * (i - 2) + g + 1))
                    pe.wait_ge(diag_done, GS * (NG * (i - 2) + g) + k + 1)
                    st = first and k == 0
                    mm(bank(va, 0), diag[:, k, :], v_ring[:, k, 0:512], st)
                    mm(bank(va, 1), diag[:, k, :], v_ring[:, k, 512:1024], st).then_inc(v_used, 1)

            def four(dst, lhs, rhs):
                for h in range(GH):
                    last = mm(heads(dst, 4)[:, h, :], heads(lhs, 4)[:, h, :], heads(rhs, 4)[:, h, :])
                return last

            def mixing(b, i, v, loop):
                t0 = steps_before(b)
                pe.wait_ge(g_split, b + 1)
                mm(bank(ox, 1)[:, 0:4], upto[:, :], ab_in[:, 0:4])
                mm(bank(ox, 1)[:, 4:12], ones[:, :], g_sel).then_inc(g_summed, 1)
                fill(i, 0, v, first=True)
                pe.wait_ge(diags_ready, b + 1)
                mm(bank(zz, 0), ones[:, :], t_xt)
                mm(bank(zz, 1), ones[:, :], t_p).then_inc(spread_done, 1)
                four(bank(rr, 0), gkT, gkT)
                four(bank(rr, 1), gkT, gqT).then_inc(pairs_done, 1)
                pe.wait_ge(tt_first, b + 1)
                turn(bank(ox, 1), t_TT, 4).then_inc(tt_turned, 1)
                fill(i, 1, v)
                for lv in range(1, 6):
                    pe.wait_ge(x_ready, 5 * b + lv)
                    if lv == 1:
                        pe.wait_ge(tt_copied, b + 1)
                    else:
                        pe.wait_ge(t_ready, 5 * b + lv - 1)
                    four(bank(zz, 0), t_xt, t_T).then_inc(p_done, 1)
                    pe.wait_ge(p_copied, 5 * b + lv)
                    if lv < 5:
                        four(bank(zz, 1), t_TT, t_p)
                    four(bank(rr, 0), t_p, t_TT).then_inc(corr_done, 1)
                    fill(i, 1 + lv, v)
                pe.wait_ge(t_ready, 5 * b + 5)
                four(bank(rr, 1), t_TT, t_vb)
                four(bank(ox, 1), t_kbg, t_TT).then_inc(uw_done, 1)
                og = bank(ox, 0)
                pe.wait_ge(uw_copied, b + 1)
                for c in range(2):
                    r = slice(64 * c, 64 * c + 64)
                    if c:
                        pe.wait_ge(state_ready, 2 * b + 1)
                    for h in range(GH):
                        last = mm(heads(bank(zz, 0), 4)[r, h, :], heads(t_wT, 4)[:, h, r], heads(state, 4)[:, h, :])
                    last.then_inc(ws_done, 1)
                    for h in range(GH):
                        mm(heads(og, 4)[r, h, :], heads(t_qd, 4)[:, h, r], heads(state, 4)[:, h, :], h == 0, False)
                    pe.wait_ge(vn_ready, 2 * b + c + 1)
                    for h in range(GH):
                        last = mm(heads(bank(zz, 1), 4)[:, h, :], heads(t_kd, 4)[r, h, :], heads(t_vn, 4)[r, h, :])
                    last.then_inc(kv_done, 1)
                    fill(i, 7 + c, v)
                for h in range(GH):
                    last = mm(heads(og, 4)[:, h, :], heads(t_dt, 4)[:, h, :], heads(t_vn, 4)[:, h, :], False, h == GH - 1)
                last.then_inc(og_done, 1)
                pe.wait_ge(state_ready, 2 * b + 2)
                pe.wait_ge(og_copied, b + 1)

                def key_step(t, g, first=False):
                    if first:
                        pe.wait_ge(q_landed, 16 * (b + 1))
                    pe.wait_ge(k_landed, 16 * (t + 1))
                    for hg in range(2):
                        pe.wait_ge(z_used[hg], t)
                        r = slice(64 * hg, 64 * hg + 64)
                        for h in range(4):
                            last = mm(heads(bank(zz, hg), 4)[:, h, :], heads(kTj, 4)[r, h, :], heads(qT, 4)[r, h, :])
                        last.then_inc(z_done[hg], 1)
                    fill(i, g, v, slots=range(2))
                    for hg in range(2):
                        pe.wait_ge(sp_done[hg], t + 1)
                        mm(bank(rr, hg), later[:, :], att_sp[hg], first, True).then_inc(later_done[hg], 1)
                    fill(i, g, v, slots=range(2, 3))
                    for hg in range(2):
                        pe.wait_ge(arg_done[hg], t + 1)
                        mm(bank(rr, hg), rest[:, :], att_sp[hg], False, True).then_inc(rest_done[hg], 1)
                    fill(i, g, v, slots=range(3, GS))
                    for hg in range(2):
                        pe.wait_ge(vj_landed, 16 * (t + 1))
                        pe.wait_ge(w_done[hg], t + 1)
                        for h in range(4):
                            c = (2 * h + hg) * SBD
                            last = mm(bank(ox, 0)[:, c:c + SBD], heads(att_u[hg], 4)[:, h, :], vj[:, c:c + SBD],
                                      first and hg == 0 and h == 0, False)
                        last.then_inc(pv_done[hg], 1)

                key_step(t0, 9, first=True)
                loop(pe, b, lambda t: key_step(t0 + t, 9 + t))
                g = 10 + b
                fill(i, g, v)
                pe.wait_ge(mix_done, b + 1)
                turn(rr[:, :], mix, KC).then_inc(mix_turned, 1)
                pe.wait_ge(mixT_act, b + 1)
                pe.wait_ge(mixT_dve, b + 1)
                if isinstance(b, int) and b == 0:
                    pe.wait_ge(wout_scaled, 1)
                    pe.wait_ge(wq_landed, 16)
                for n in range(2):
                    for k in range(KC):
                        last = mm(bank(zz, n), mixT[:, k * P:(k + 1) * P], w_out_sb[:, k, n * HALF:(n + 1) * HALF],
                                  k == 0, k == KC - 1)
                last.then_inc(out_done, 1)
                fill(i, g + 1, v)
                pe.wait_ge(hn_done, b + 1)
                turn(rr[:, :], hn_new, KC).then_inc(hn_turned, 1)
                fill(i, g + 2, v)
                pe.wait_ge(hnT_act, b + 1)
                pe.wait_ge(hnT_dve, b + 1)
                pair = (zz, rr)
                for q in range(4):
                    for c in range(4):
                        col = (4 * q + c) * P
                        for k in range(KC):
                            last = mm(heads(bank(pair[q // 2], q % 2), 4)[:, c, :], w_q_sb[:, k, col:col + P],
                                      hnT[:, k * P:(k + 1) * P], k == 0, k == KC - 1)
                    last.then_inc(pq_done, 1)
                    fill(i, g + 3 + q, v)
                pe.wait_ge(sub_in_b, 16 * (b + 1))
                for q in range(4):
                    pe.wait_ge(pq_copied, 4 * b + q + 1)
                    for c in range(4):
                        last = mm(heads(bank(pair[q // 2], q % 2), 4)[:, c, :], pqT[:, 4 * q + c, :], subT[:, 4 * q + c, :])
                    last.then_inc(sc_done, 1)
                for q in range(7):
                    fill(i, g + 7 + q, v)
                pe.wait_ge(sc_copied, 4 * b + 4)
                return g + 14

            def rest_groups(i, g):
                if isinstance(g, int) and g == 0:
                    fill(i, 0, True, first=True)
                    g = 1
                with pe.Fori(g, NG) as gg:
                    fill(i, gg, True)
                count = settled(pe, i - 1)
                known(pe)
                pe.wait_ge(y_done, count)

            mixing(0, 0, False, py_loop)
            mixing(1, 1, False, py_loop)
            with pe.Fori(2, NB) as i:
                rest_groups(i, mixing(i, i, True, fori_loop))
            rest_groups(NB, 0)
            rest_groups(NB + 1, 0)


_INS = ["x", "norm1_w", "w_in", "sb_q_norm_w", "sb_k_norm_w", "sb_out_norm_w", "gdn_conv_w", "gdn_a_log",
        "gdn_dt_bias", "gdn_out_norm_w", "w_out", "norm2_w", "peer_w_q", "peer_sub_keys_1", "peer_sub_keys_2",
        "peer_u", "peer_v"]


def kernel(**inputs):
    import concourse.bacc as bacc
    import numpy as np
    from concourse.bass_utils import run_bass_kernel_spmd

    nc = bacc.Bacc("TRN2", target_bir_lowering=False, num_devices=1)
    arrays, args = {}, []
    for name in _INS:
        a = np.ascontiguousarray(inputs[name])
        arrays[f"in_{name}"] = a
        args.append(nc.dram_tensor(f"in_{name}", a.shape, mybir.dt.from_np(a.dtype), kind="ExternalInput").ap())
    out = nc.dram_tensor("out_y", (1, S, D), F32, kind="ExternalOutput").ap()
    hybrid_layer_kernel(nc, *args, out)
    r = run_bass_kernel_spmd(nc, [arrays], core_ids=[0])
    return r.results[0]["out_y"]
```
